# Optimizing a Trainium2 kernel written in Bass

```python
import jax, jax.numpy as jnp
from jax import lax
import numpy as np
import math

D_MODEL = 1024
BATCH = 1
SEQ = 512
DEPTH = 2

HEAD_DIM = 64
SWA_HEADS = 8
SWA_KV_HEADS = 2
SWA_WINDOW = 128
SWA_BLOCK = SWA_WINDOW
RWKV_HEADS = 8
RWKV_DIM = RWKV_HEADS * HEAD_DIM
RWKV_W_LORA = 64
RWKV_A_LORA = 64
RWKV_G_LORA = 128
RWKV_GN_EPS = 64e-5
NSA_HEADS = 16
NSA_KV_HEADS = 4
CMP_LEN = 32
CMP_STRIDE = 16
CMP_HIDDEN = 256
SEL_LEN = 64
N_SEL = 8
NSA_WINDOW = 256
NSA_QBLOCK = 64
N_BRANCH = 3
D_FF = 2816
CONV_WIDTH = 3
NORM_EPS = 1e-6

N_EVEN = (DEPTH + 1) // 2
N_ODD = DEPTH // 2

SWA_Q_COLS = SWA_HEADS * HEAD_DIM
SWA_KV_COLS = SWA_KV_HEADS * HEAD_DIM
SWA_COLS = SWA_Q_COLS + 2 * SWA_KV_COLS
RWKV_SPLITS = (RWKV_DIM, RWKV_DIM, RWKV_DIM, RWKV_W_LORA, RWKV_A_LORA, RWKV_G_LORA)
RWKV_COLS = sum(RWKV_SPLITS)
HY_COLS = SWA_COLS + RWKV_COLS
HY_OUT = SWA_Q_COLS + RWKV_DIM
NSA_KV_COLS = NSA_KV_HEADS * HEAD_DIM
NSA_SPLITS = (NSA_HEADS * HEAD_DIM,) + (NSA_KV_COLS,) * 6 + (NSA_HEADS * N_BRANCH,)
NSA_COLS = sum(NSA_SPLITS)
NSA_OUT = NSA_HEADS * HEAD_DIM


def split_cols(z, sizes):
    return jnp.split(z, [int(c) for c in np.cumsum(sizes)[:-1]], axis=-1)

def rms_norm(x, g):
    xf = x.astype(jnp.float32)
    y = xf * lax.rsqrt(jnp.mean(xf * xf, axis=-1, keepdims=True) + NORM_EPS)
    return (y * g.astype(jnp.float32)).astype(x.dtype)

def alibi_slopes(n_heads):
    return jnp.exp2(-8.0 * jnp.arange(1, n_heads + 1, dtype=jnp.float32) / n_heads)

def masked_softmax(s, valid):
    s = jnp.where(valid, s, -jnp.inf)
    m = jnp.max(s, axis=-1, keepdims=True)
    m = jnp.where(jnp.isfinite(m), m, 0.0)
    p = jnp.where(valid, jnp.exp(s - m), 0.0)
    d = jnp.sum(p, axis=-1, keepdims=True)
    return p / jnp.where(d > 0, d, 1.0)

def swa_sink_attention(q, k, v, sinks, slopes):
    B, T, _ = q.shape
    G, H, D, L = SWA_KV_HEADS, SWA_HEADS, HEAD_DIM, SWA_BLOCK
    R = H // G
    nb = T // L
    f32 = jnp.float32
    qb = q.reshape(B, nb, L, G, R, D).astype(f32) * D ** -0.5

    def band(a):
        a = jnp.pad(a.reshape(B, T, G, D), ((0, 0), (L, 0), (0, 0), (0, 0))).reshape(B, nb + 1, L, G, D)
        return jnp.concatenate([a[:, :-1], a[:, 1:]], axis=2).astype(f32)

    kb, vb = band(k), band(v)
    qpos = jnp.arange(nb)[:, None, None] * L + jnp.arange(L)[None, :, None]
    kpos = jnp.arange(nb)[:, None, None] * L - L + jnp.arange(2 * L)[None, None, :]
    dist = qpos - kpos
    valid = (dist >= 0) & (dist < SWA_WINDOW) & (kpos >= 0)
    s = jnp.einsum('bnqgrd,bnkgd->bngrqk', qb, kb)
    s = s - slopes.reshape(G, R)[None, None, :, :, None, None] * dist.astype(f32)[None, :, None, None]
    s = jnp.where(valid[None, :, None, None], s, -jnp.inf)
    sink = sinks.astype(f32).reshape(G, R)[None, None, :, :, None, None]
    m = jnp.maximum(jnp.max(s, axis=-1, keepdims=True), sink)
    p = jnp.exp(s - m)
    p = p / (jnp.sum(p, axis=-1, keepdims=True) + jnp.exp(sink - m))
    o = jnp.einsum('bngrqk,bnkgd->bnqgrd', p, vb)
    return o.reshape(B, T, H * D)

def rwkv7_time_mix(z, mu, w0, w2, a0, a2, g2, k_k, k_a, r_k, ln_g, ln_b):
    B, T, _ = z.shape
    H, N = RWKV_HEADS, HEAD_DIM
    f32 = jnp.float32
    z_prev = jnp.pad(z, ((0, 0), (1, 0), (0, 0)))[:, :-1]
    z = z + (z_prev - z) * mu
    r, k, v, w_lo, a_lo, g_lo = split_cols(z, RWKV_SPLITS)
    log_w = -jax.nn.softplus(-(w0 + jnp.tanh(w_lo) @ w2).astype(f32)) - 0.5
    decay = jnp.exp(-jnp.exp(log_w))
    a = jax.nn.sigmoid((a0 + a_lo @ a2).astype(f32))
    g = (jax.nn.sigmoid(g_lo) @ g2).astype(f32)
    heads = lambda t: t.astype(f32).reshape(B, T, H, N)
    r, k, v, decay, a = heads(r), heads(k), heads(v), heads(decay), heads(a)
    kk = k * k_k.astype(f32).reshape(H, N)
    kk = kk / jnp.maximum(jnp.linalg.norm(kk, axis=-1, keepdims=True), 1e-12)
    k = k * (1.0 + (a - 1.0) * k_a.astype(f32).reshape(H, N))

    def step(S, inp):
        r_t, w_t, k_t, v_t, kk_t, a_t = inp
        sa = jnp.einsum('bhij,bhj->bhi', S, kk_t)
        S = S * w_t[:, :, None, :] - sa[..., None] * (kk_t * a_t)[:, :, None, :] + v_t[..., None] * k_t[:, :, None, :]
        return S, jnp.einsum('bhij,bhj->bhi', S, r_t)

    seq = tuple(jnp.moveaxis(t, 1, 0) for t in (r, decay, k, v, kk, a))
    _, y = lax.scan(step, jnp.zeros((B, H, N, N), f32), seq)
    y = jnp.moveaxis(y, 0, 1)
    mean = jnp.mean(y, axis=-1, keepdims=True)
    var = jnp.mean(jnp.square(y - mean), axis=-1, keepdims=True)
    y = ((y - mean) * lax.rsqrt(var + RWKV_GN_EPS)).reshape(B, T, RWKV_DIM)
    y = y * ln_g.astype(f32) + ln_b.astype(f32)
    bonus = jnp.sum(r * k * r_k.astype(f32), axis=-1, keepdims=True) * v
    return (y + bonus.reshape(B, T, RWKV_DIM)) * g

def hybrid_swa_rwkv(h, w_in, w_out, sinks, mu, w0, w2, a0, a2, g2, k_k, k_a, r_k, ln_g, ln_b):
    z = h @ w_in
    q, k, v = split_cols(z[..., :SWA_COLS], (SWA_Q_COLS, SWA_KV_COLS, SWA_KV_COLS))
    o_a = swa_sink_attention(q, k, v, sinks, alibi_slopes(SWA_HEADS))
    o_b = rwkv7_time_mix(z[..., SWA_COLS:], mu, w0, w2, a0, a2, g2, k_k, k_a, r_k, ln_g, ln_b)
    o = jnp.concatenate([o_a, o_b], axis=-1).astype(h.dtype)
    return o @ w_out

def compress_blocks(a, idx, pos, w1, w2):
    blocks = a[:, idx] + pos[None, None, :, None, :]
    hdn = jax.nn.gelu(jnp.einsum('bclgd,ldf->bcgf', blocks, w1), approximate=True)
    return jnp.einsum('bcgf,fd->bcgd', hdn, w2)

def nsa_layer(h, w_in, w_out, pos_k, w1_k, w2_k, pos_v, w1_v, w2_v):
    B, T, _ = h.shape
    G, H, D = NSA_KV_HEADS, NSA_HEADS, HEAD_DIM
    R = H // G
    Q = NSA_QBLOCK
    f32 = jnp.float32
    z = h @ w_in
    q, kc, vc, ks, vs, kw, vw, gl = split_cols(z, NSA_SPLITS)
    q = q.reshape(B, T, G, R, D).astype(f32) * D ** -0.5
    kv = lambda t: t.reshape(B, T, G, D)
    kc, vc, ks, vs, kw, vw = kv(kc), kv(vc), kv(ks), kv(vs), kv(kw), kv(vw)
    gates = jax.nn.sigmoid(gl.astype(f32)).reshape(B, T, G, R, N_BRANCH)
    slopes = alibi_slopes(H).reshape(G, R)

    n_cmp = (T - CMP_LEN) // CMP_STRIDE + 1
    cmp_idx = np.arange(n_cmp)[:, None] * CMP_STRIDE + np.arange(CMP_LEN)[None, :]
    k_cmp = compress_blocks(kc, cmp_idx, pos_k, w1_k, w2_k).astype(f32)
    v_cmp = compress_blocks(vc, cmp_idx, pos_v, w1_v, w2_v).astype(f32)
    cmp_end = jnp.asarray(cmp_idx[:, -1], jnp.int32)

    n_blk = T // SEL_LEN
    k_sel = min(N_SEL, n_blk)
    ks_blk = ks.reshape(B, n_blk, SEL_LEN, G, D).transpose(0, 3, 1, 2, 4).astype(f32)
    vs_blk = vs.reshape(B, n_blk, SEL_LEN, G, D).transpose(0, 3, 1, 2, 4).astype(f32)
    ratio, span = SEL_LEN // CMP_STRIDE, CMP_LEN // CMP_STRIDE
    ov = (ratio * np.arange(n_blk)[:, None, None] + np.arange(ratio)[None, :, None]
          - np.arange(span)[None, None, :]).reshape(n_blk, ratio * span)
    ov_valid = jnp.asarray((ov >= 0) & (ov < n_cmp), f32)
    ov = jnp.asarray(np.clip(ov, 0, n_cmp - 1), jnp.int32)
    blk_ids = jnp.arange(n_blk)
    b_ix = jnp.arange(B)[:, None, None, None]
    g_ix = jnp.arange(G)[None, :, None, None]

    kw_pad = jnp.pad(kw, ((0, 0), (NSA_WINDOW, 0), (0, 0), (0, 0))).astype(f32)
    vw_pad = jnp.pad(vw, ((0, 0), (NSA_WINDOW, 0), (0, 0), (0, 0))).astype(f32)

    def block(i):
        t0 = i * Q
        t = t0 + jnp.arange(Q)
        qi = lax.dynamic_slice_in_dim(q, t0, Q, axis=1)
        g_blk = lax.dynamic_slice_in_dim(gates, t0, Q, axis=1)
        dist_c = t[:, None] - cmp_end[None, :]
        s = jnp.einsum('bqgrd,bcgd->bgrqc', qi, k_cmp) - slopes[:, :, None, None] * dist_c.astype(f32)
        p_cmp = masked_softmax(s, dist_c >= 0)
        o_cmp = jnp.einsum('bgrqc,bcgd->bqgrd', p_cmp, v_cmp)
        imp = jnp.sum(jnp.sum(p_cmp, axis=2)[..., ov] * ov_valid, axis=-1)
        cur = (t // SEL_LEN)[:, None]
        forced = (blk_ids == 0) | (blk_ids == cur) | (blk_ids == cur - 1)
        imp = jnp.where(forced, jnp.inf, jnp.where(blk_ids > cur, -jnp.inf, imp))
        _, sel = lax.top_k(imp, k_sel)
        k_g = ks_blk[b_ix, g_ix, sel]
        v_g = vs_blk[b_ix, g_ix, sel]
        kpos = sel[..., None] * SEL_LEN + jnp.arange(SEL_LEN)
        dist_s = (t[:, None, None] - kpos)[:, :, None]
        s = jnp.einsum('bqgrd,bgqnkd->bgrqnk', qi, k_g) - slopes[None, :, :, None, None, None] * dist_s.astype(f32)
        p = masked_softmax(s.reshape(B, G, R, Q, k_sel * SEL_LEN), (dist_s >= 0).reshape(B, G, 1, Q, k_sel * SEL_LEN))
        o_slc = jnp.einsum('bgrqnk,bgqnkd->bqgrd', p.reshape(s.shape), v_g)
        kwi = lax.dynamic_slice_in_dim(kw_pad, t0, NSA_WINDOW + Q, axis=1)
        vwi = lax.dynamic_slice_in_dim(vw_pad, t0, NSA_WINDOW + Q, axis=1)
        kp = t0 - NSA_WINDOW + jnp.arange(NSA_WINDOW + Q)
        dist_w = t[:, None] - kp[None, :]
        valid_w = (dist_w >= 0) & (dist_w < NSA_WINDOW) & (kp[None, :] >= 0)
        s = jnp.einsum('bqgrd,bkgd->bgrqk', qi, kwi) - slopes[:, :, None, None] * dist_w.astype(f32)
        o_win = jnp.einsum('bgrqk,bkgd->bqgrd', masked_softmax(s, valid_w), vwi)
        return g_blk[..., 0, None] * o_cmp + g_blk[..., 1, None] * o_slc + g_blk[..., 2, None] * o_win

    o = lax.map(block, jnp.arange(T // Q))
    o = jnp.moveaxis(o, 0, 1).reshape(B, T, NSA_OUT).astype(h.dtype)
    return o @ w_out

def conv_ffn(h, w_up, conv_w, conv_b, w_down):
    T = h.shape[1]
    gate, val = jnp.split(h @ w_up, 2, axis=-1)
    gp = jnp.pad(gate, ((0, 0), (CONV_WIDTH - 1, 0), (0, 0)))
    conv = conv_b + gp[:, CONV_WIDTH - 1:] * conv_w[CONV_WIDTH - 1]
    for j in range(CONV_WIDTH - 1):
        conv = conv + gp[:, j:j + T] * conv_w[j]
    return (jax.nn.gelu(conv, approximate=True) * val) @ w_down

def first_inputs(seed: int = 0) -> dict:
    key = jax.random.key(seed)
    keys = iter(jax.random.split(key, 48))
    f32 = jnp.float32
    nrm = lambda shape, scale: jax.random.normal(next(keys), shape, f32) * scale
    uni = lambda shape, lo, hi: jax.random.uniform(next(keys), shape, f32, lo, hi)
    NE, NO = N_EVEN, N_ODD
    return {
        "x": nrm((BATCH, SEQ, D_MODEL), 1.0),
        "mix_pre_g": 1.0 + nrm((DEPTH, D_MODEL), 0.05),
        "mix_post_g": 1.0 + nrm((DEPTH, D_MODEL), 0.05),
        "ffn_pre_g": 1.0 + nrm((DEPTH, D_MODEL), 0.05),
        "ffn_post_g": 1.0 + nrm((DEPTH, D_MODEL), 0.05),
        "hy_w_in": nrm((NE, D_MODEL, HY_COLS), D_MODEL ** -0.5),
        "hy_w_out": nrm((NE, HY_OUT, D_MODEL), HY_OUT ** -0.5),
        "swa_sinks": nrm((NE, SWA_HEADS), 0.5),
        "rwkv_mu": uni((NE, RWKV_COLS), 0.0, 1.0),
        "rwkv_w0": uni((NE, RWKV_DIM), -5.0, -1.0),
        "rwkv_w2": nrm((NE, RWKV_W_LORA, RWKV_DIM), 0.1),
        "rwkv_a0": nrm((NE, RWKV_DIM), 0.1),
        "rwkv_a2": nrm((NE, RWKV_A_LORA, RWKV_DIM), 0.1),
        "rwkv_g2": nrm((NE, RWKV_G_LORA, RWKV_DIM), RWKV_G_LORA ** -0.5),
        "rwkv_k_k": 0.85 + nrm((NE, RWKV_DIM), 0.05),
        "rwkv_k_a": 1.0 + nrm((NE, RWKV_DIM), 0.05),
        "rwkv_r_k": nrm((NE, RWKV_HEADS, HEAD_DIM), 0.1),
        "rwkv_ln_g": 1.0 + nrm((NE, RWKV_DIM), 0.05),
        "rwkv_ln_b": nrm((NE, RWKV_DIM), 0.01),
        "nsa_w_in": nrm((NO, D_MODEL, NSA_COLS), D_MODEL ** -0.5),
        "nsa_w_out": nrm((NO, NSA_OUT, D_MODEL), NSA_OUT ** -0.5),
        "nsa_cmp_pos_k": nrm((NO, CMP_LEN, HEAD_DIM), 0.1),
        "nsa_cmp_w1_k": nrm((NO, CMP_LEN, HEAD_DIM, CMP_HIDDEN), (CMP_LEN * HEAD_DIM) ** -0.5),
        "nsa_cmp_w2_k": nrm((NO, CMP_HIDDEN, HEAD_DIM), CMP_HIDDEN ** -0.5),
        "nsa_cmp_pos_v": nrm((NO, CMP_LEN, HEAD_DIM), 0.1),
        "nsa_cmp_w1_v": nrm((NO, CMP_LEN, HEAD_DIM, CMP_HIDDEN), (CMP_LEN * HEAD_DIM) ** -0.5),
        "nsa_cmp_w2_v": nrm((NO, CMP_HIDDEN, HEAD_DIM), CMP_HIDDEN ** -0.5),
        "ffn_w_up": nrm((DEPTH, D_MODEL, 2 * D_FF), D_MODEL ** -0.5),
        "ffn_conv_w": nrm((DEPTH, CONV_WIDTH, D_FF), CONV_WIDTH ** -0.5),
        "ffn_conv_b": nrm((DEPTH, D_FF), 0.01),
        "ffn_w_down": nrm((DEPTH, D_FF, D_MODEL), D_FF ** -0.5),
    }

def first_block(x, mix_pre_g, mix_post_g, ffn_pre_g, ffn_post_g, hy_w_in, hy_w_out, swa_sinks,
              rwkv_mu, rwkv_w0, rwkv_w2, rwkv_a0, rwkv_a2, rwkv_g2, rwkv_k_k, rwkv_k_a, rwkv_r_k,
              rwkv_ln_g, rwkv_ln_b, nsa_w_in, nsa_w_out, nsa_cmp_pos_k, nsa_cmp_w1_k, nsa_cmp_w2_k,
              nsa_cmp_pos_v, nsa_cmp_w1_v, nsa_cmp_w2_v, ffn_w_up, ffn_conv_w, ffn_conv_b, ffn_w_down):
    for layer in range(DEPTH):
        i = layer // 2
        h = rms_norm(x, mix_pre_g[layer])
        if layer % 2 == 0:
            m = hybrid_swa_rwkv(h, hy_w_in[i], hy_w_out[i], swa_sinks[i], rwkv_mu[i], rwkv_w0[i],
                                rwkv_w2[i], rwkv_a0[i], rwkv_a2[i], rwkv_g2[i], rwkv_k_k[i],
                                rwkv_k_a[i], rwkv_r_k[i], rwkv_ln_g[i], rwkv_ln_b[i])
        else:
            m = nsa_layer(h, nsa_w_in[i], nsa_w_out[i], nsa_cmp_pos_k[i], nsa_cmp_w1_k[i],
                          nsa_cmp_w2_k[i], nsa_cmp_pos_v[i], nsa_cmp_w1_v[i], nsa_cmp_w2_v[i])
        x = x + rms_norm(m, mix_post_g[layer])
        h = rms_norm(x, ffn_pre_g[layer])
        x = x + rms_norm(conv_ffn(h, ffn_w_up[layer], ffn_conv_w[layer], ffn_conv_b[layer], ffn_w_down[layer]),
                         ffn_post_g[layer])
    return x


DEPTH_2 = 1

HEAD_DIM_2 = 128
HEADS_PER_GROUP = 4
DILATED_GROUPS = ((128, 1), (512, 4), (2048, 16))
N_GROUPS = 3
N_ATTN_HEADS = N_GROUPS * HEADS_PER_GROUP
ATTN_QKV_WIDTH = N_ATTN_HEADS * HEAD_DIM_2
ATTN_OUT_WIDTH = HEADS_PER_GROUP * HEAD_DIM_2
BAND_BLOCK = 128
LRU_WIDTH = D_MODEL
LRU_HEADS = 4
LRU_HEAD_DIM = LRU_WIDTH // LRU_HEADS
CONV_WIDTH_2 = 4
LRU_C = 8.0
REL_BUCKETS = 32
REL_MAX_DISTANCE = 2048
N_BRANCHES = 2
W_IN_COLS = 3 * ATTN_QKV_WIDTH + 2 * LRU_WIDTH + N_BRANCHES * D_MODEL


def rms_norm_2(x, g):
    xf = x.astype(jnp.float32)
    y = xf * lax.rsqrt(jnp.mean(xf * xf, axis=-1, keepdims=True) + NORM_EPS)
    return (y * g.astype(jnp.float32)).astype(x.dtype)

def swiglu(x, w_gate, w_up, w_down):
    return (jax.nn.silu(x @ w_gate) * (x @ w_up)) @ w_down

def t5_causal_bucket(distance):
    max_exact = REL_BUCKETS // 2
    nf = jnp.maximum(distance, 1).astype(jnp.float32)
    large = max_exact + (jnp.log(nf / max_exact) / math.log(REL_MAX_DISTANCE / max_exact)
                         * (REL_BUCKETS - max_exact)).astype(jnp.int32)
    large = jnp.minimum(large, REL_BUCKETS - 1)
    return jnp.where(distance < max_exact, distance, large)

def dilated_group_attention(q, k, v, bias_table_g, window, dilation):
    B, S, H, E = q.shape
    d = dilation
    L = S // d
    nb = -(-L // BAND_BLOCK)
    Lp = nb * BAND_BLOCK
    m_max = window // d

    def to_blocks(t):
        t = t.reshape(B, L, d, H, E)
        t = jnp.pad(t, ((0, 0), (0, Lp - L), (0, 0), (0, 0), (0, 0)))
        return t.reshape(B, nb, BAND_BLOCK, d, H, E)

    def band(t):
        tb = jnp.pad(to_blocks(t), ((0, 0), (1, 0), (0, 0), (0, 0), (0, 0), (0, 0)))
        return jnp.concatenate([tb[:, :-1], tb[:, 1:]], axis=2)

    qb = to_blocks(q)
    kb = band(k)
    vb = band(v)

    qi = jnp.arange(BAND_BLOCK)[:, None]
    kj = jnp.arange(2 * BAND_BLOCK)[None, :]
    steps = qi + BAND_BLOCK - kj
    key_idx = jnp.arange(nb)[:, None, None] * BAND_BLOCK - BAND_BLOCK + kj[None]
    valid = (steps >= 0) & (steps <= m_max) & (key_idx >= 0)
    bucket = t5_causal_bucket(jnp.maximum(steps, 0) * d)
    bias = jnp.transpose(bias_table_g[bucket], (2, 0, 1)).astype(jnp.float32)

    scale = 1.0 / math.sqrt(E)
    scores = jnp.einsum('bnqphe,bnkphe->bphnqk', qb, kb).astype(jnp.float32) * scale
    scores = scores + bias[None, None, :, None]
    scores = jnp.where(valid[None, None, None], scores, -jnp.inf)
    mx = jnp.max(scores, axis=-1, keepdims=True)
    e = jnp.exp(scores - mx)
    den = jnp.sum(e, axis=-1, keepdims=True)
    o = jnp.einsum('bphnqk,bnkphe->bnqphe', (e / den).astype(v.dtype), vb)
    lse = (mx + jnp.log(den))[..., 0]
    o = o.reshape(B, Lp, d, H, E)[:, :L].reshape(B, S, H, E)
    lse = jnp.transpose(lse, (0, 3, 4, 1, 2)).reshape(B, Lp, d, H)[:, :L].reshape(B, S, H)
    return o, lse

def rg_lru_branch(xr, conv_w, conv_b, w_x, b_x, w_a, b_a, a_param):
    B, S, C = xr.shape
    xc = lax.conv_general_dilated(
        xr, conv_w[:, None, :].astype(xr.dtype), window_strides=(1,),
        padding=((CONV_WIDTH_2 - 1, 0),), dimension_numbers=('NWC', 'WIO', 'NWC'),
        feature_group_count=C) + conv_b
    xh = xc.reshape(B, S, LRU_HEADS, LRU_HEAD_DIM)
    gate_x = jax.nn.sigmoid(jnp.einsum('bshi,hij->bshj', xh, w_x) + b_x).reshape(B, S, C)
    gate_a = jax.nn.sigmoid(jnp.einsum('bshi,hij->bshj', xh, w_a) + b_a).reshape(B, S, C)
    log_a = -LRU_C * gate_a.astype(jnp.float32) * jax.nn.softplus(-a_param.astype(jnp.float32))
    a = jnp.exp(log_a)
    b = jnp.sqrt(-jnp.expm1(2.0 * log_a)) * (gate_x * xc).astype(jnp.float32)

    def combine(left, right):
        a_l, b_l = left
        a_r, b_r = right
        return a_l * a_r, a_r * b_l + b_r

    _, h = lax.associative_scan(combine, (a, b), axis=1)
    return h.astype(xr.dtype)

def second_inputs(seed: int = 0) -> dict:
    key = jax.random.key(seed)
    ks = jax.random.split(key, 32)
    f32 = jnp.float32

    def w(k, shape, fan_in):
        return jax.random.normal(k, shape, f32) * (fan_in ** -0.5)

    def gain(k):
        return 1.0 + 0.05 * jax.random.normal(k, (DEPTH_2, D_MODEL), f32)

    a0 = jax.random.uniform(ks[20], (DEPTH_2, LRU_WIDTH), f32, 0.9, 0.999)
    s = a0 ** (1.0 / LRU_C)
    a_param = jnp.log(s) - jnp.log1p(-s)

    return {
        "x": jax.random.normal(ks[0], (BATCH, SEQ, D_MODEL), f32),
        "ffn1_norm_pre": gain(ks[1]),
        "ffn1_norm_post": gain(ks[2]),
        "ffn1_w_gate": w(ks[3], (DEPTH_2, D_MODEL, D_FF), D_MODEL),
        "ffn1_w_up": w(ks[4], (DEPTH_2, D_MODEL, D_FF), D_MODEL),
        "ffn1_w_down": w(ks[5], (DEPTH_2, D_FF, D_MODEL), D_FF),
        "mix_norm_pre": gain(ks[6]),
        "mix_norm_post": gain(ks[7]),
        "w_in": w(ks[8], (DEPTH_2, D_MODEL, W_IN_COLS), D_MODEL),
        "rel_bias_table": 0.2 * jax.random.normal(ks[9], (REL_BUCKETS, N_ATTN_HEADS), f32),
        "conv_w": w(ks[10], (DEPTH_2, CONV_WIDTH_2, LRU_WIDTH), CONV_WIDTH_2),
        "conv_b": 0.02 * jax.random.normal(ks[11], (DEPTH_2, LRU_WIDTH), f32),
        "lru_w_x": w(ks[12], (DEPTH_2, LRU_HEADS, LRU_HEAD_DIM, LRU_HEAD_DIM), LRU_HEAD_DIM),
        "lru_b_x": 0.02 * jax.random.normal(ks[13], (DEPTH_2, LRU_HEADS, LRU_HEAD_DIM), f32),
        "lru_w_a": w(ks[14], (DEPTH_2, LRU_HEADS, LRU_HEAD_DIM, LRU_HEAD_DIM), LRU_HEAD_DIM),
        "lru_b_a": 0.02 * jax.random.normal(ks[15], (DEPTH_2, LRU_HEADS, LRU_HEAD_DIM), f32),
        "lru_a_param": a_param,
        "w_attn_branch": w(ks[16], (DEPTH_2, ATTN_OUT_WIDTH, D_MODEL), ATTN_OUT_WIDTH),
        "w_rec_branch": w(ks[17], (DEPTH_2, LRU_WIDTH, D_MODEL), LRU_WIDTH),
        "w_out": w(ks[18], (DEPTH_2, D_MODEL, D_MODEL), D_MODEL),
        "ffn2_norm_pre": gain(ks[21]),
        "ffn2_norm_post": gain(ks[22]),
        "ffn2_w_gate": w(ks[23], (DEPTH_2, D_MODEL, D_FF), D_MODEL),
        "ffn2_w_up": w(ks[24], (DEPTH_2, D_MODEL, D_FF), D_MODEL),
        "ffn2_w_down": w(ks[25], (DEPTH_2, D_FF, D_MODEL), D_FF),
    }

def second_block(x, ffn1_norm_pre, ffn1_norm_post, ffn1_w_gate, ffn1_w_up, ffn1_w_down,
              mix_norm_pre, mix_norm_post, w_in, rel_bias_table, conv_w, conv_b,
              lru_w_x, lru_b_x, lru_w_a, lru_b_a, lru_a_param,
              w_attn_branch, w_rec_branch, w_out,
              ffn2_norm_pre, ffn2_norm_post, ffn2_w_gate, ffn2_w_up, ffn2_w_down):
    B, S, _ = x.shape
    splits = [ATTN_QKV_WIDTH, 2 * ATTN_QKV_WIDTH, 3 * ATTN_QKV_WIDTH,
              3 * ATTN_QKV_WIDTH + LRU_WIDTH, 3 * ATTN_QKV_WIDTH + 2 * LRU_WIDTH]
    h = x
    for l in range(DEPTH_2):
        f = swiglu(rms_norm_2(h, ffn1_norm_pre[l]), ffn1_w_gate[l], ffn1_w_up[l], ffn1_w_down[l])
        h = h + 0.5 * rms_norm_2(f, ffn1_norm_post[l])

        u = rms_norm_2(h, mix_norm_pre[l])
        proj = u @ w_in[l]
        q, k, v, xr, yr, gl = jnp.split(proj, splits, axis=-1)
        q = q.reshape(B, S, N_GROUPS, HEADS_PER_GROUP, HEAD_DIM_2)
        k = k.reshape(B, S, N_GROUPS, HEADS_PER_GROUP, HEAD_DIM_2)
        v = v.reshape(B, S, N_GROUPS, HEADS_PER_GROUP, HEAD_DIM_2)

        outs, lses = [], []
        for g, (window, dilation) in enumerate(DILATED_GROUPS):
            o_g, lse_g = dilated_group_attention(
                q[:, :, g], k[:, :, g], v[:, :, g],
                rel_bias_table[:, g * HEADS_PER_GROUP:(g + 1) * HEADS_PER_GROUP],
                window, dilation)
            outs.append(o_g)
            lses.append(lse_g)
        alpha = jax.nn.softmax(jnp.stack(lses, axis=0), axis=0)
        attn = jnp.einsum('gbsh,gbshe->bshe', alpha, jnp.stack(outs, axis=0).astype(jnp.float32))
        attn_d = attn.astype(x.dtype).reshape(B, S, ATTN_OUT_WIDTH) @ w_attn_branch[l]

        rec = rg_lru_branch(xr, conv_w[l], conv_b[l], lru_w_x[l], lru_b_x[l],
                            lru_w_a[l], lru_b_a[l], lru_a_param[l]) * jax.nn.gelu(yr)
        rec_d = rec @ w_rec_branch[l]

        gates = jax.nn.sigmoid(gl).reshape(B, S, N_BRANCHES, D_MODEL)
        merged = gates[:, :, 0] * attn_d + gates[:, :, 1] * rec_d
        h = h + rms_norm_2(merged @ w_out[l], mix_norm_post[l])

        f = swiglu(rms_norm_2(h, ffn2_norm_pre[l]), ffn2_w_gate[l], ffn2_w_up[l], ffn2_w_down[l])
        h = h + 0.5 * rms_norm_2(f, ffn2_norm_post[l])
    return h


def setup_inputs(seed=0):
    out = dict(first_inputs(seed))
    for name, value in second_inputs(seed + 1).items():
        if name != "x":
            out[name + "_2"] = value
    return out


def reference(
    x, mix_pre_g, mix_post_g, ffn_pre_g, ffn_post_g, hy_w_in, hy_w_out, swa_sinks, rwkv_mu,
    rwkv_w0, rwkv_w2, rwkv_a0, rwkv_a2, rwkv_g2, rwkv_k_k, rwkv_k_a, rwkv_r_k, rwkv_ln_g,
    rwkv_ln_b, nsa_w_in, nsa_w_out, nsa_cmp_pos_k, nsa_cmp_w1_k, nsa_cmp_w2_k, nsa_cmp_pos_v,
    nsa_cmp_w1_v, nsa_cmp_w2_v, ffn_w_up, ffn_conv_w, ffn_conv_b, ffn_w_down, ffn1_norm_pre_2,
    ffn1_norm_post_2, ffn1_w_gate_2, ffn1_w_up_2, ffn1_w_down_2, mix_norm_pre_2,
    mix_norm_post_2, w_in_2, rel_bias_table_2, conv_w_2, conv_b_2, lru_w_x_2, lru_b_x_2,
    lru_w_a_2, lru_b_a_2, lru_a_param_2, w_attn_branch_2, w_rec_branch_2, w_out_2,
    ffn2_norm_pre_2, ffn2_norm_post_2, ffn2_w_gate_2, ffn2_w_up_2, ffn2_w_down_2,
):
    x = first_block(
        x, mix_pre_g, mix_post_g, ffn_pre_g, ffn_post_g, hy_w_in, hy_w_out, swa_sinks, rwkv_mu,
        rwkv_w0, rwkv_w2, rwkv_a0, rwkv_a2, rwkv_g2, rwkv_k_k, rwkv_k_a, rwkv_r_k, rwkv_ln_g,
        rwkv_ln_b, nsa_w_in, nsa_w_out, nsa_cmp_pos_k, nsa_cmp_w1_k, nsa_cmp_w2_k,
        nsa_cmp_pos_v, nsa_cmp_w1_v, nsa_cmp_w2_v, ffn_w_up, ffn_conv_w, ffn_conv_b, ffn_w_down,
    )
    return second_block(
        x, ffn1_norm_pre_2, ffn1_norm_post_2, ffn1_w_gate_2, ffn1_w_up_2, ffn1_w_down_2,
        mix_norm_pre_2, mix_norm_post_2, w_in_2, rel_bias_table_2, conv_w_2, conv_b_2,
        lru_w_x_2, lru_b_x_2, lru_w_a_2, lru_b_a_2, lru_a_param_2, w_attn_branch_2,
        w_rec_branch_2, w_out_2, ffn2_norm_pre_2, ffn2_norm_post_2, ffn2_w_gate_2, ffn2_w_up_2,
        ffn2_w_down_2,
    )


_drawn_inputs = setup_inputs


def setup_inputs(seed=0):
    import zlib

    import numpy as np

    out = dict(_drawn_inputs(seed))
    spreads = {}
    factors = {'swa_sinks': 3.041,
     'rwkv_ln_b': 4.396,
     'nsa_cmp_pos_k': 8.0,
     'ffn_conv_b': 6.283,
     'ffn1_norm_pre_2': 3.357,
     'ffn1_norm_post_2': 4.923,
     'mix_norm_post_2': 2.749,
     'rel_bias_table_2': 3.701,
     'lru_b_x_2': 8.0,
     'lru_b_a_2': 23.339,
     'ffn2_norm_pre_2': 4.065,
     'ffn2_norm_post_2': 6.075}
    for name, (base, spread) in spreads.items():
        noise = np.random.default_rng([zlib.crc32(name.encode()), seed]).standard_normal(out[name].shape)
        drawn = base * np.exp(spread * noise) if base else spread * noise
        out[name] = __import__('jax').numpy.asarray(drawn.astype(out[name].dtype))
    for name, factor in factors.items():
        out[name] = (out[name] * factor).astype(out[name].dtype)
    return out
```

```python
from contextlib import ExitStack

import numpy as np
import concourse.bass as bass
from concourse import mybir

F32 = mybir.dt.float32
F32R = mybir.dt.float32r
ALU = mybir.AluOpType
ACT = mybir.ActivationFunctionType
AX = mybir.AxisListType

P = 128
T = 512
D = 1024
KD = D // P
D_FF = 2816
KF = D_FF // P
EPS = 1e-6
SLOTS = 4
PAIRS = 2
BANKS = 4
NBMAX = KF // 2
BIG = 1.0e30


class Product:

    def __init__(self, k, name, tiles, kt, x_hi, x_lo, ktile=None):
        self.upt = 2 if kt > NBMAX else 1
        self.nb = kt // self.upt
        self.name, self.tiles, self.units = name, tiles, tiles * self.upt
        self.w, self.x_hi, self.x_lo = k.w[name], x_hi, x_lo
        self.u0, self.n0 = k.units, k.tiles
        k.units += self.units
        k.tiles += tiles
        k.nb += [self.nb] * self.units
        self.loops, self.rest = divmod(tiles, BANKS)

    def part(self, t):
        return self.nb, self.x_hi, self.x_lo

    def source(self, j, i, step):
        return self.w[j] if isinstance(i, int) else self.w[bass.ds(i * step + j, 1)].rearrange("o p n -> (o p) n")

    def bank(self, t):
        return (self.n0 + t) % BANKS

    def last_unit(self, t):
        return self.u0 + (t + 1) * self.upt - 1

    def end(self):
        return self.u0 + self.units + PAIRS


class Kit:

    def __init__(self, nc, w, vec, cols):
        self.nc, self.w, self.vec, self.cols = nc, w, vec, cols
        self.units = self.tiles = 0
        self.nb = []
        self.phases = []
        self.input_events = 0
        self.update_events = 0
        self.feed_forwards = self.convs = 0
        self.at_items = self.at_exps = self.at_units = self.values_turned = self.outs_turned = 0

    def v(self, name, t=0, n=1):
        c = self.cols[name]
        return self.vec[:, bass.ds(t + c, n)] if not isinstance(t, int) else self.vec[:, c + t:c + t + n]

    def sp_product(self, sp, g):
        def load(j, i, step):
            u = g.u0 + j
            sp.wait_ge(self.lo_done, u + 1 + i * step)
            sp.dma_start(self.raw[u % SLOTS][:, 0:self.nb[u] * P], g.source(j, i, step)).then_inc(self.raw_in[u % SLOTS], 16)

        step = BANKS * g.upt
        if g.loops:
            with sp.Fori(0, g.loops) as i:
                for j in range(step):
                    load(j, i, step)
        for j in range(g.loops * step, g.units):
            load(j, 0, 0)

    def hi(self, act, u, off=0):
        if u >= self.units:
            return
        n = self.nb[u] * P
        act.wait_ge(self.raw_in[u % SLOTS], (u // SLOTS + 1) * 16 + off * (16 // SLOTS))
        act.wait_ge(self.mm, u + 1 + off)
        act.activation(self.w_hi[u % PAIRS][:, 0:n], self.raw[u % SLOTS][:, 0:n], ACT.Copy).then_inc(self.hi_done, 1)

    def act_product(self, act, g, tile):
        step = BANKS * g.upt

        def body(t0, i, off):
            for t in range(t0, min(t0 + BANKS, g.tiles)):
                for q in range(g.upt):
                    self.hi(act, g.u0 + t * g.upt + q + PAIRS, off)
                tile(t, i)

        if g.loops > 1:
            with act.Fori(0, g.loops - 1) as i:
                body(0, i, i * step)
        if g.loops:
            body((g.loops - 1) * BANKS, 0, 0)
        if g.rest:
            body(g.loops * BANKS, 0, 0)

    def pool_product(self, pool, g):
        def low(j, i, step):
            u = g.u0 + j
            n = self.nb[u] * P
            pool.wait_ge(self.hi_done, u + 1 + i * step)
            pool.tensor_tensor(self.w_lo[u % PAIRS][:, 0:n], self.raw[u % SLOTS][:, 0:n],
                               self.w_hi[u % PAIRS][:, 0:n].bitcast(F32), ALU.subtract).then_inc(self.lo_done, 1)

        step = BANKS * g.upt
        if g.loops:
            with pool.Fori(0, g.loops) as i:
                for j in range(step):
                    low(j, i, step)
        for j in range(g.loops * step, g.units):
            low(j, 0, 0)

    def pe_tile(self, pe, g, t, i=0):
        bank = self.gb[g.bank(t)]
        nb, x_hi, x_lo = g.part(t)
        for q in range(g.upt):
            u = g.u0 + t * g.upt + q
            pe.wait_ge(self.lo_done, u + 1 + SLOTS + i * (BANKS * g.upt))
            if q == 0:
                pe.wait_ge(self.bank_free, g.n0 + t + 1 + i * BANKS)
            hi, lo = self.w_hi[u % PAIRS], self.w_lo[u % PAIRS]
            for b in range(nb):
                k = q * nb + b
                c = slice(b * P, (b + 1) * P)
                first, final = k == 0, k == nb * g.upt - 1
                pe.matmul(bank[:], hi[:, c], x_hi[:, k], start=first, stop=False)
                pe.matmul(bank[:], hi[:, c], x_lo[:, k], start=False, stop=False)
                mm = pe.matmul(bank[:], lo[:, c], x_hi[:, k], start=False, stop=final)
            mm.then_inc(self.mm, 1)

    def pe_product(self, pe, g):
        if g.loops:
            with pe.Fori(0, g.loops) as i:
                for t in range(BANKS):
                    self.pe_tile(pe, g, t, i)
        for t in range(g.loops * BANKS, g.tiles):
            self.pe_tile(pe, g, t)

    def tile_ready(self, eng, g, t, i=0):
        eng.wait_ge(self.mm, g.last_unit(t) + 1 + PAIRS + i * (BANKS * g.upt))

    def sweep(self, eng, g, tile):
        if g.loops:
            with eng.Fori(0, g.loops) as i:
                for t in range(BANKS):
                    tile(t, i)
        for t in range(g.loops * BANKS, g.tiles):
            tile(t, 0)


def no_part(*_):
    pass


class Phase:
    def __init__(self, sp=no_part, act=no_part, pool=no_part, pe=no_part, dve=no_part):
        self.sp, self.act, self.pool, self.pe, self.dve = sp, act, pool, pe, dve


def pre_norm(k, gain, sem, wait_x, free):
    squares, stat, root, scaled, done = (sem(f"pre_{n}") for n in ("squares", "stat", "root", "scaled", "hi"))
    bank = k.ab[0]
    e = k.input_events
    k.input_events += 1
    n0, r0 = e * KD, e * 2

    def act(act):
        for t in range(KD):
            wait_x(act, t)
            if t >= 2:
                act.wait_ge(stat, n0 + t - 1)
            act.activation(k.sq[t % 2][:], k.x[:, t], ACT.Square).then_inc(squares, 1)
        act.wait_ge(stat, n0 + KD)
        act.activation(k.ln[:], bank[:], ACT.Ln, bias=k.eps[:, 0:1], scale=1.0 / D).then_inc(root, 1)
        act.wait_ge(root, r0 + 1)
        act.activation(k.r[:], k.ln[:], ACT.Exp, scale=-0.5).then_inc(root, 1)
        act.wait_ge(k.mm, free)
        for t in range(KD):
            act.wait_ge(scaled, n0 + t + 1)
            act.activation(k.x_hi[:, t], k.ht[t % 2][:], ACT.Copy).then_inc(done, 1)

    def pe(pe):
        for t in range(KD):
            pe.wait_ge(squares, n0 + t + 1)
            pe.matmul(bank[:], k.ones[:], k.sq[t % 2][:], start=t == 0, stop=t == KD - 1).then_inc(stat, 1)

    def dve(dve):
        dve.wait_ge(root, r0 + 2)
        dve.wait_ge(k.mm, free)
        for t in range(KD):
            if t >= 2:
                dve.wait_ge(k.input_ready, n0 + t - 1)
            dve.scalar_tensor_tensor(out=k.ht[t % 2][:], in0=k.x[:, t], scalar=k.v(gain, t), in1=k.r[:],
                                     op0=ALU.mult, op1=ALU.mult).then_inc(scaled, 1)
            if t >= 1:
                lo(dve, t - 1)
        lo(dve, KD - 1)

    def lo(dve, t):
        dve.wait_ge(done, n0 + t + 1)
        dve.tensor_tensor(k.x_lo[:, t], k.ht[t % 2][:], k.x_hi[:, t].bitcast(F32),
                          ALU.subtract).then_inc(k.input_ready, 1)

    return Phase(act=act, pe=pe, dve=dve)


def post_norm(k, g, m, gain, sem, wait_input):
    squared, summed, stat, root, term = (sem(f"post_{n}") for n in
                                         ("squared", "summed", "stat", "root", "term"))
    bank = k.ab[1]
    e = k.update_events
    k.update_events += 1
    n0, s0 = e * KD, e * (KD + 2)

    def col(t, i):
        return m[:, t] if isinstance(i, int) else m[:, bass.ds(i * BANKS + t, 1)].rearrange("p o n -> p (o n)")

    def act(act):
        def tile(t, i):
            act.wait_ge(k.bank_free, g.n0 + BANKS + t + 1 + i * BANKS)
            act.wait_ge(summed, s0 + 1 + t + i * BANKS)
            act.activation(k.sq[t % 2][:], col(t, i), ACT.Square).then_inc(squared, 1)

        k.act_product(act, g, tile)
        act.wait_ge(stat, e + 1)
        act.activation(k.ln[:], bank[:], ACT.Ln, bias=k.eps[:, 0:1], scale=1.0 / D).then_inc(root, 1)
        act.wait_ge(root, 2 * e + 1)
        act.activation(k.r[:], k.ln[:], ACT.Exp, scale=-0.5).then_inc(root, 1)

    def pe(pe):
        wait_input(pe)
        k.pe_product(pe, g)
        pe.wait_ge(summed, s0 + g.tiles + 2)
        pe.matmul(bank[:], k.ones[:], k.acc[:], start=True, stop=True).then_inc(stat, 1)

    def dve(dve):
        dve.memset(k.acc[:], 0.0).then_inc(summed, 2)

        def tile(t, i):
            k.tile_ready(dve, g, t, i)
            dve.tensor_copy(col(t, i), k.gb[g.bank(t)][:]).then_inc(k.bank_free, 1)
            dve.wait_ge(squared, n0 + t + 1 + i * BANKS)
            dve.wait_ge(summed, s0 + t + 2 + i * BANKS)
            dve.tensor_tensor(k.acc[:], k.acc[:], k.sq[t % 2][:], ALU.add).then_inc(summed, 1)

        k.sweep(dve, g, tile)
        dve.wait_ge(root, 2 * e + 2)
        dve.wait_ge(k.bank_free, g.n0 + BANKS + g.tiles)
        for t in range(KD):
            if t >= 2:
                dve.wait_ge(k.x_updated, n0 + t - 1)
            dve.scalar_tensor_tensor(out=k.ht[t % 2][:], in0=m[:, t], scalar=k.v(gain, t), in1=k.r[:],
                                     op0=ALU.mult, op1=ALU.mult).then_inc(term, 1)
            if t >= 1:
                add(dve, t - 1)
        add(dve, KD - 1)

    def add(dve, t):
        dve.wait_ge(term, n0 + t + 1)
        dve.tensor_tensor(k.x[:, t], k.x[:, t], k.ht[t % 2][:], ALU.add).then_inc(k.x_updated, 1)

    return Phase(sp=lambda sp: k.sp_product(sp, g), act=act, pool=lambda pool: k.pool_product(pool, g), pe=pe, dve=dve)


def ffn_up(k, name, mem, sem, conv=None):
    g = Product(k, name, 2 * KF, KD, k.x_hi, k.x_lo)
    e = k.input_events
    f = k.feed_forwards
    k.feed_forwards += 1
    n0, p0, v0 = f * KF, f * (KF + 2), k.convs * KF
    k.convs += 1 if conv else 0
    first, tap1, tap2, opened, product, high, low = (
        sem(f"up_{n}") for n in ("first", "tap1", "tap2", "opened", "product", "high", "low"))
    c, h_hi, h_lo = mem.c, mem.h_hi, mem.h_lo

    def col(h, t, i):
        return h[:, t] if isinstance(i, int) else h[:, bass.ds(i * 2 + t, 1)].rearrange("p o n -> p (o n)")

    def act(act):
        def tile(t, i):
            p, bank = t // 2, k.gb[g.bank(t)]
            if t % 2 == 0:
                k.tile_ready(act, g, t, i)
                act.wait_ge(product, p0 + 1 + p + i * 2)
                if conv:
                    act.activation(c[p % 2][:], bank[:], ACT.Identity, bias=k.v(conv + "_b", p + i * 2),
                                   scale=k.v(conv + "_w2", p + i * 2)).then_inc(first, 1)
                else:
                    act.activation(c[p % 2][:], bank[:], ACT.Silu).then_inc(opened, 1)
            else:
                if conv:
                    act.wait_ge(tap2, v0 + p + 1 + i * 2)
                    act.activation(c[p % 2][:], c[p % 2][:], ACT.Gelu_apprx_tanh).then_inc(opened, 1)
                act.wait_ge(product, p0 + 3 + p + i * 2)
                act.activation(col(h_hi, p, i), k.ht[p % 2][:], ACT.Copy).then_inc(high, 1)

        k.act_product(act, g, tile)

    def pe(pe):
        pe.wait_ge(k.input_ready, e * KD)
        k.pe_product(pe, g)

    def dve(dve):
        dve.sem_inc(product, 2)
        dve.sem_inc(low, 2)

        def tile(t, i):
            p, bank = t // 2, k.gb[g.bank(t)]
            if t % 2 == 0:
                if conv:
                    dve.wait_ge(first, v0 + p + 1 + i * 2)
                    dve.scalar_tensor_tensor(out=c[p % 2][:, 1:T], in0=bank[:, 0:T - 1], scalar=k.v(conv + "_w1", p + i * 2),
                                             in1=c[p % 2][:, 1:T], op0=ALU.mult, op1=ALU.add).then_inc(tap1, 1)
                    dve.wait_ge(tap1, v0 + p + 1 + i * 2)
                    dve.scalar_tensor_tensor(out=c[p % 2][:, 2:T], in0=bank[:, 0:T - 2], scalar=k.v(conv + "_w0", p + i * 2),
                                             in1=c[p % 2][:, 2:T], op0=ALU.mult, op1=ALU.add).then_inc(tap2, 1)
            else:
                dve.wait_ge(opened, n0 + p + 1 + i * 2)
                k.tile_ready(dve, g, t, i)
                dve.wait_ge(low, p0 + p + 1 + i * 2)
                dve.tensor_tensor(k.ht[p % 2][:], c[p % 2][:], bank[:], ALU.mult).then_inc(product, 1)
                dve.wait_ge(high, n0 + p + 1 + i * 2)
                dve.wait_ge(product, p0 + p + 3 + i * 2)
                dve.sem_inc(k.bank_free, 2)
                dve.tensor_tensor(col(h_lo, p, i), k.ht[p % 2][:], col(h_hi, p, i).bitcast(F32),
                                  ALU.subtract).then_inc(low, 1)

        k.sweep(dve, g, tile)

    phase = Phase(sp=lambda sp: k.sp_product(sp, g), act=act, pool=lambda pool: k.pool_product(pool, g), pe=pe, dve=dve)
    phase.g = g
    phase.h_ready = lambda eng: eng.wait_ge(low, p0 + KF + 2)
    return phase


def feed_forward(k, up, down, mem, gain_pre, gain_post, sem, wait_x, free, conv=None):
    k.phases.append(pre_norm(k, gain_pre, sem, wait_x, free))
    first = ffn_up(k, up, mem, sem, conv)
    k.phases.append(first)
    g = Product(k, down, KD, KF, mem.h_hi, mem.h_lo)
    k.phases.append(post_norm(k, g, mem.m, gain_post, sem, first.h_ready))
    return g.end()


HD = 64
CH = 64
TT = T // P
DECAY = float(np.exp(-0.5))
GN_EPS = 64e-5


def shifted_product(k, name, tiles, z, keep_scale, mu, sem):
    g = Product(k, name, tiles, KD, k.x_hi, k.x_lo)
    e = k.input_events
    scaled = sem("z_scaled")

    def col(t, i, lo=0):
        return z[:, t, lo:T] if isinstance(i, int) else z[:, bass.ds(i * BANKS + t, 1), lo:T].rearrange("p o n -> p (o n)")

    def act(act):
        def tile(t, i):
            k.tile_ready(act, g, t, i)
            act.activation(col(t, i), k.gb[g.bank(t)][:], ACT.Identity, scale=keep_scale(t + i * BANKS)).then_inc(scaled, 1)

        k.act_product(act, g, tile)

    def pe(pe):
        pe.wait_ge(k.input_ready, e * KD)
        k.pe_product(pe, g)

    def dve(dve):
        def tile(t, i):
            dve.wait_ge(scaled, t + 1 + i * BANKS)
            dve.scalar_tensor_tensor(out=col(t, i, 1), in0=k.gb[g.bank(t)][:, 0:T - 1], scalar=mu(t + i * BANKS),
                                     in1=col(t, i, 1), op0=ALU.mult, op1=ALU.add).then_inc(k.bank_free, 1)

        k.sweep(dve, g, tile)

    phase = Phase(sp=lambda sp: k.sp_product(sp, g), act=act, pool=lambda pool: k.pool_product(pool, g), pe=pe, dve=dve)
    phase.g = g
    return phase


def rwkv_prelude(k, z, mem, ready, sem):
    low, gate, pw, pa, sigd, siga, sqk, ssk, norm, normc, lnn, inv, unit, cum, prev, p, ip, pp, kf, kk2, rk, bs, bon, b, b2, k2, a2, r2, kraw, pcs = (
        sem(f"rw_{n}") for n in ("low", "gate", "pw", "pa", "sigd", "siga", "sqk", "ssk", "norm", "normc", "lnn", "inv",
                                 "unit", "cum", "prev", "p", "ip", "pp", "kf", "kk2", "rk", "bs", "bon", "b", "b2", "k2",
                                 "a2", "r2", "kraw", "pcs"))
    zr, zk, zv = (z[:, 6 + 4 * j:10 + 4 * j] for j in range(3))
    wide = [k.db[j] for j in range(4)]

    def act(act):
        ready(act)
        act.wait_ge(mem.loaded, 16 * mem.n_loads)
        act.activation(z[0:HD, 18], z[0:HD, 18], ACT.Tanh).then_inc(low, 1)
        act.activation(mem.sg[:], z[:, 19], ACT.Sigmoid).then_inc(gate, 1)
        for t in range(4):
            act.wait_ge(pw, t + 1)
            act.activation(mem.ld[:, t], wide[t][:, 0], ACT.Sigmoid, bias=k.v("w0", t)).then_inc(sigd, 1)
            act.wait_ge(pa, t + 1)
            act.activation(mem.b[:, t], wide[t][:, 1], ACT.Sigmoid, bias=k.v("a0", t)).then_inc(siga, 1)
        for t in range(4):
            if t >= 2:
                act.wait_ge(ssk, t - 1)
            act.activation(k.sq[t % 2][:], zk[:, t], ACT.Square, scale=k.v("k_k", t)).then_inc(sqk, 1)
        for t in range(4):
            act.wait_ge(ssk, t + 1)
            act.activation(mem.a[:, t], wide[t][:, 0], ACT.Sqrt).then_inc(norm, 1)
        for t in range(4):
            act.wait_ge(normc, t + 1)
            act.activation(mem.a[:, t], mem.a[:, t], ACT.Ln).then_inc(lnn, 1)
        for t in range(4):
            act.wait_ge(lnn, t + 1)
            act.activation(mem.a[:, t], mem.a[:, t], ACT.Exp, scale=-1.0).then_inc(inv, 1)
        for t in range(4):
            act.wait_ge(cum, t + 1)
            act.activation(mem.e1[:, t], mem.l[:, t], ACT.Exp, scale=-DECAY).then_inc(p, 1)
            act.wait_ge(prev, t + 1)
            act.activation(mem.ld[:, t], mem.ld[:, t], ACT.Exp, scale=-DECAY).then_inc(pp, 1)
            act.wait_ge(p, t + 1)
            act.activation(mem.l[:, t], mem.l[:, t], ACT.Exp, scale=DECAY).then_inc(ip, 1)

    def pe(pe):
        ready(pe)
        pe.wait_ge(mem.loaded, 16 * mem.n_loads)
        pe.wait_ge(low, 1)
        for t in range(4):
            c = slice(t * P, (t + 1) * P)
            pe.matmul(wide[t][:, 0], mem.wa2[0:HD, c], z[0:HD, 18], start=True, stop=True).then_inc(pw, 1)
            pe.matmul(wide[t][:, 1], mem.wa2[HD:P, c], z[HD:P, 18], start=True, stop=True).then_inc(pa, 1)
        for t in range(4):
            pe.wait_ge(sqk, t + 1)
            pe.wait_ge(siga, t + 1)
            pe.matmul(wide[t][:, 0], k.bones[:], k.sq[t % 2][:], start=True, stop=True).then_inc(ssk, 1)
        for t in range(4):
            pe.wait_ge(rk, t + 1)
            pe.matmul(wide[t][:, 1], k.bones[:], k.ht[t % 2][:], start=True, stop=True).then_inc(bs, 1)

    def dve(dve):
        ready(dve)
        dve.wait_ge(mem.loaded, 16 * mem.n_loads)
        for t in range(4):
            dve.wait_ge(sigd, t + 1)
            dve.tensor_tensor_scan(mem.l[:, t], mem.keep[:], mem.ld[:, t], 0.0, ALU.mult, ALU.add).then_inc(cum, 1)
        for t in range(4):
            dve.wait_ge(cum, t + 1)
            dve.tensor_tensor(mem.ld[:, t], mem.l[:, t], mem.ld[:, t], ALU.subtract).then_inc(prev, 1)
        for t in range(4):
            dve.wait_ge(norm, t + 1)
            dve.tensor_scalar(mem.a[:, t], mem.a[:, t], 1e-12, None, ALU.max).then_inc(normc, 1)
        for t in range(4):
            dve.wait_ge(siga, t + 1)
            dve.wait_ge(bon if t >= 2 else siga, t - 1 if t >= 2 else 1)
            dve.tensor_scalar(k.ht[t % 2][:], mem.b[:, t], k.v("k_a", t), k.v("one_k_a", t), ALU.mult, ALU.add).then_inc(kf, 1)
            dve.wait_ge(inv, t + 1)
            dve.scalar_tensor_tensor(out=mem.a[:, t], in0=zk[:, t], scalar=k.v("k_k", t), in1=mem.a[:, t],
                                     op0=ALU.mult, op1=ALU.mult).then_inc(unit, 1)
            dve.wait_ge(kf, t + 1)
            dve.wait_ge(unit, t + 1)
            dve.tensor_tensor(zk[:, t], zk[:, t], k.ht[t % 2][:], ALU.mult).then_inc(kk2, 1)
            dve.wait_ge(kk2, t + 1)
            dve.scalar_tensor_tensor(out=k.ht[t % 2][:], in0=zr[:, t], scalar=k.v("r_k", t), in1=zk[:, t],
                                     op0=ALU.mult, op1=ALU.mult).then_inc(rk, 1)
            dve.tensor_tensor(mem.b[:, t], mem.b[:, t], mem.a[:, t], ALU.mult).then_inc(b, 1)
            dve.wait_ge(ip, t + 1)
            dve.wait_ge(b, t + 1)
            dve.tensor_tensor(mem.b[:, t], mem.b[:, t], mem.l[:, t], ALU.mult).then_inc(b2, 1)
            dve.scalar_tensor_tensor(out=mem.a[:, t], in0=mem.a[:, t], scalar=-1.0, in1=mem.ld[:, t],
                                     op0=ALU.mult, op1=ALU.mult).then_inc(b2, 1)
            dve.wait_ge(rk, t + 1)
            dve.tensor_tensor(zk[:, t], zk[:, t], mem.l[:, t], ALU.mult).then_inc(b2, 1)
            dve.tensor_tensor(zr[:, t], zr[:, t], mem.e1[:, t], ALU.mult).then_inc(b2, 1)
            dve.wait_ge(bs, t + 1)
            dve.tensor_tensor(mem.bonus[:, t], wide[t][:, 1], zv[:, t], ALU.mult).then_inc(bon, 1)
        dve.tensor_copy(mem.pc[:], mem.e1[:].rearrange("p t (c n) -> p t c n", n=CH)[:, :, :, CH - 1]).then_inc(b2, 1)

    def done(eng):
        eng.wait_ge(b2, 17)

    phase = Phase(act=act, pe=pe, dve=dve)
    phase.done, phase.bonus_done = done, lambda eng: eng.wait_ge(bon, 4)
    return phase


class Stage:

    def __init__(self, name, needs, matmuls, takes):
        self.name, self.needs, self.matmuls, self.takes = name, needs, matmuls, takes


def rwkv_core(k, z, mem, before, sem):
    made, taken = sem("core_made"), {e: sem(f"core_taken_{e}") for e in ("act", "dve", "pool")}
    zk, zr, zv = z[:, 10:14], z[:, 6:10], z[:, 14:18]
    m = mem
    stages = []

    def head(buf, h):
        hh = (h % 2) * 4 + h // 2
        return buf[:, hh * P:(hh + 1) * P]

    def half(buf, h, part):
        return head(buf, h)[:, part * HD:(part + 1) * HD]

    def fm(f, h, tt):
        return f[(h % 2) * HD:(h % 2 + 1) * HD, h // 2, tt * P:(tt + 1) * P]

    def square(lhs, rhs):
        def mms(pe, db):
            for h in range(8):
                mm = pe.matmul(db[:, h % 2, (h // 2) * P:(h // 2 + 1) * P], head(lhs, h), head(rhs, h), start=True, stop=True)
            return mm
        return mms

    def cross(f, g, tt):
        def mms(pe, db):
            for h in range(8):
                mm = pe.matmul(db[:, h % 2, (h // 2) * P:(h // 2 + 1) * P], fm(f, h, tt), fm(g, h, tt), start=True, stop=True)
            return mm
        return mms

    def flat(db):
        return db.rearrange("p a n -> p (a n)")

    def heads(ap):
        return ap.rearrange("p (h n) -> p h n", h=8)

    def masked(out, mask):
        return lambda e, db: e.tensor_tensor(heads(out[:]), heads(flat(db)), mask[:].unsqueeze(1).to_broadcast([P, 8, P]), ALU.mult)

    def copied(out):
        return lambda e, db: e.activation(out[:], flat(db), ACT.Copy)

    def added(out, to):
        return lambda e, db: e.tensor_tensor(out[:], flat(db), to[:], ALU.add)

    def turned(f, tt):
        def mms(pe, db):
            for c in range(4):
                mm = pe.transpose(db[:, 0, c * P:(c + 1) * P], f[:, c, tt * P:(tt + 1) * P], k.ident[:])
            return mm
        return mms

    def by_tile(db):
        return db[:, 0].rearrange("p (c e n) -> p c e n", c=4, e=2)

    def in_heads(buf, n):
        return buf[:].rearrange("p (e c n) -> p c e n", e=2, c=4)[:, :, :, 0:n]

    def add_tt(tt):
        def st(name, needs, mms, *takes):
            stages.append(Stage(f"{name}{tt}", [f"{n}{tt}" for n in needs], mms, takes))

        def spread(buf, src_of):
            def one(c):
                r = slice(c * HD, (c + 1) * HD)
                return lambda e, db: e.tensor_copy(
                    buf[:].rearrange("p (h c n) -> p h c n", h=8, c=2)[r, :, c, :], src_of(r))
            return ("pool", one(0)), ("pool", one(1))

        st("L", [], cross(m.a, m.b, tt), ("dve", masked(m.d, k.mask["d"])), ("dve", masked(m.lo, k.mask["lo"])))
        st("Lt", [], cross(m.b, m.a, tt), ("dve", masked(m.dt, k.mask["dt"])),
           ("dve", lambda e, db: e.tensor_tensor(heads(m.i1[:]), heads(m.dt[:]), k.ident[:].unsqueeze(1).to_broadcast([P, 8, P]), ALU.add)))
        st("Lak", [], cross(zk, m.a, tt), ("dve", masked(m.ak, k.mask["upper"])))
        st("At", [], turned(m.a, tt), ("act", lambda e, db: e.activation(in_heads(m.x0, HD), by_tile(db), ACT.Copy)))
        st("Vt", [], turned(zv, tt), ("act", lambda e, db: e.activation(in_heads(m.vt, HD), by_tile(db), ACT.Copy)),
           *spread(m.v_bd, lambda r: m.vt[:].rearrange("p (h n) -> p h n", h=8)[r]))
        st("Bt", [], turned(m.b, tt), ("act", lambda e, db: e.activation(in_heads(m.bt, HD), by_tile(db), ACT.Copy)),
           *spread(m.b_bd, lambda r: m.bt[:].rearrange("p (h n) -> p h n", h=8)[r]))
        st("Kt", [], turned(zk, tt), ("act", lambda e, db: e.activation(in_heads(m.kt, HD), by_tile(db), ACT.Copy)))
        st("D2", ["L", "Lt"], square(m.dt, m.d), ("act", copied(m.d2)))
        st("D2t", ["L", "Lt"], square(m.d, m.dt), ("act", copied(m.d2t)))

        def lv(pe, db):
            for h in range(8):
                hh = (h % 2) * 4 + h // 2
                mm = pe.matmul(db[:, 0, hh * HD:(hh + 1) * HD], head(m.ak, h), m.vt[:, hh * HD:(hh + 1) * HD], start=True, stop=True)
            return mm
        st("LV", ["Lak", "Vt"], lv, ("act", lambda e, db: e.activation(
            heads(m.x0[:])[:, :, HD:P], db[:, 0].rearrange("p (h n) -> p h n", h=8), ACT.Copy)))
        st("I2", ["D2", "Lt"], square(m.d2, m.i1), ("dve", added(m.i2, m.i1)))
        st("D4", ["D2", "D2t"], square(m.d2t, m.d2), ("act", copied(m.d)))
        st("D4t", ["D2", "D2t"], square(m.d2, m.d2t), ("act", copied(m.dt)))
        st("I3", ["D4", "I2"], square(m.d, m.i2), ("dve", added(m.i1, m.i2)))
        st("D8", ["D4", "D4t"], square(m.dt, m.d), ("act", copied(m.d2)))
        st("I4", ["D8", "I3"], square(m.d2, m.i1), ("dve", added(m.i2, m.i1)))
        st("N", ["I4", "L"], square(m.i2, m.lo), ("act", copied(m.d)))
        st("Nt", ["I4", "L"], square(m.lo, m.i2), ("act", copied(m.dt)))
        st("X1", ["I4", "LV", "At"], square(m.i2, m.x0), ("act", copied(m.x1)))
        st("Mrb", [], cross(m.b, zr, tt), ("dve", masked(m.ak, k.mask["upto"])))
        st("N2t", ["N", "Nt"], square(m.d, m.dt), ("act", copied(m.d2)))
        st("Mrk", [], cross(zk, zr, tt), ("dve", masked(m.d2t, k.mask["upto"])))
        st("X2", ["N2t", "X1"], square(m.d2, m.x1), ("dve", added(m.x0, m.x1)))
        st("X3", ["Nt", "X2"], square(m.dt, m.x0), ("dve", added(m.x1, m.x0)),
           *spread(m.tv_bd, lambda r: heads(m.x1[:])[r, :, HD:P]))

        def rows(*pairs):
            def mms(pe, db):
                for h in range(8):
                    for n, (lhs, rhs) in enumerate(pairs):
                        mm = pe.matmul(db[(h % 2) * HD:(h % 2 + 1) * HD, 0, (h // 2) * P:(h // 2 + 1) * P],
                                       lhs(h), rhs(h), start=n == 0, stop=n == len(pairs) - 1)
                return mm
            return mms

        def narrow(buf):
            return lambda h: buf[:, ((h % 2) * 4 + h // 2) * HD:((h % 2) * 4 + h // 2 + 1) * HD]

        def gt(part):
            r = slice(part * HD, (part + 1) * HD)
            return lambda e, db: e.tensor_tensor(
                m.gt[:].rearrange("p (t c e n) -> p t c e n", t=4, c=2, e=2)[r, :, :, part, :].rearrange("p t c n -> p (t c) n"),
                db[r, 0].rearrange("p (t n) -> p t n", n=HD),
                k.eye2[r, :].unsqueeze(1).to_broadcast([HD, 8, HD]), ALU.add)
        st("G", ["X3", "Bt"], rows((lambda h: half(m.x1, h, 0), lambda h: head(m.b_bd, h))), ("dve", gt(0)), ("dve", gt(1)))
        st("H", ["X3", "Bt", "Kt", "Vt"], rows((narrow(m.bt), lambda h: head(m.tv_bd, h)), (narrow(m.kt), lambda h: head(m.v_bd, h))),
           ("act", lambda e, db: e.activation(m.h[:], db[:, 0], ACT.Copy)))
        tok = slice(tt * P, (tt + 1) * P)
        st("RQ", ["X3", "Mrb"], rows((lambda h: half(m.x1, h, 0), lambda h: head(m.ak, h))),
           ("dve", lambda e, db: e.tensor_tensor(m.rq[:].rearrange("p (c n) -> p c n", c=4), db[:, 0].rearrange("p (c n) -> p c n", c=4),
                                                 zr[:, :, tok], ALU.add)))
        st("Y2", ["X3", "Mrb", "Mrk", "Vt"], rows((lambda h: half(m.x1, h, 1), lambda h: head(m.ak, h)), (narrow(m.vt), lambda h: head(m.d2t, h))),
           ("act", lambda e, db: e.activation(m.y2[:], db[:, 0], ACT.Copy)))
        for c in range(2):
            ch = 2 * tt + c
            prev = f"S{ch - 1}!" if ch else None
            s_in, s_out = m.s[ch % 2], m.s[(ch + 1) % 2]

            def y1(pe, db, c=c):
                for t in range(4):
                    mm = pe.matmul(db[:, 0, t * HD:(t + 1) * HD], m.s_bd[:, t * P:(t + 1) * P],
                                   m.rq[:, t * P + c * HD:t * P + (c + 1) * HD], start=True, stop=True)
                return mm

            def s1(pe, db, c=c, s_in=s_in):
                for t in range(4):
                    mm = pe.matmul(db[:, 0, t * HD:(t + 1) * HD], m.gt[:, (2 * t + c) * P:(2 * t + c + 1) * P],
                                   s_in[:, t * HD:(t + 1) * HD], start=True, stop=True)
                return mm

            def v4(ap):
                return ap.rearrange("p (t n) -> p t n", t=4)

            def both(buf, c=c):
                return buf[:].rearrange("p (t c n) -> p t c n", t=4, c=2)[:, :, c, :]

            y_takes = [("dve", lambda e, db, c=c, ch=ch: e.tensor_tensor(
                m.y[:, :, ch * CH:(ch + 1) * CH], v4(db[:, 0, 0:4 * HD]), both(m.y2, c), ALU.add))]
            stages.append(Stage(f"Y{ch}!", [f"RQ{tt}", f"Y2{tt}"] + ([prev] if prev else []), y1, y_takes))
            s_takes = [("dve", lambda e, db, c=c: e.tensor_tensor(v4(m.tmp[:, 0:4 * HD]), v4(db[:, 0, 0:4 * HD]), both(m.h, c), ALU.add)),
                       ("dve", lambda e, db, ch=ch, s_out=s_out: e.tensor_tensor(
                           v4(s_out), v4(m.tmp[:, 0:4 * HD]), m.pc[:, :, ch:ch + 1].to_broadcast([P, 4, HD]), ALU.mult))]
            for part in range(2):
                s_takes.append(("act", lambda e, db, part=part, s_out=s_out: e.activation(
                    m.s_bd[:].rearrange("p (t e n) -> p t e n", t=4, e=2)[part * HD:(part + 1) * HD, :, part, :],
                    v4(s_out)[part * HD:(part + 1) * HD], ACT.Copy)))
            if ch < 2 * TT - 1:
                stages.append(Stage(f"S{ch}!", [f"G{tt}", f"H{tt}"] + ([prev] if prev else []), s1, s_takes))

    for tt in range(TT):
        add_tt(tt)

    count, total = {}, {"act": 0, "dve": 0, "pool": 0}
    starts = []
    for s in stages:
        starts.append(dict(total))
        for e, _ in s.takes:
            total[e] += 1
        count[s.name] = {e: total[e] for e in {e for e, _ in s.takes}}

    def pe(pe):
        before(pe)
        for e, n in m.cleared:
            pe.wait_ge(e, n)
        for n, s in enumerate(stages):
            for need in s.needs:
                for e, c in count[need].items():
                    pe.wait_ge(taken[e], c)
            if n >= 4:
                for e, c in count[stages[n - 4].name].items():
                    pe.wait_ge(taken[e], c)
            s.matmuls(pe, k.db[n % 4]).then_inc(made, 1)

    def taker(name):
        def run(eng):
            before(eng)
            for e, n in m.cleared:
                eng.wait_ge(e, n)
            for n, s in enumerate(stages):
                mine = [j for j, (e, _) in enumerate(s.takes) if e == name]
                if not mine:
                    continue
                eng.wait_ge(made, n + 1)
                seen = dict(starts[n])
                for j, (e, f) in enumerate(s.takes):
                    if e == name:
                        for o, c in seen.items():
                            if c > starts[n][o]:
                                eng.wait_ge(taken[o], c)
                        if name == "pool" and seen[name]:
                            eng.wait_ge(taken[name], seen[name])
                        f(eng, k.db[n % 4]).then_inc(taken[name], 1)
                    seen[e] += 1
            if name == "pool":
                eng.wait_ge(taken[name], total[name])
        return run

    phase = Phase(act=taker("act"), dve=taker("dve"), pool=taker("pool"), pe=pe)
    phase.done = lambda eng: [eng.wait_ge(taken[e], total[e]) for e in total]
    return phase


def rwkv_out(k, mem, before, bonus_done, sem):
    mean, centred, squared, var, root, normed, biased, gated, opened, high = (
        sem(f"gn_{n}") for n in ("mean", "centred", "squared", "var", "root", "normed", "biased", "gated", "opened", "high"))
    y = mem.y
    low = sem("gn_low")

    def pe(pe):
        before(pe)
        pe.wait_ge(mem.late, 16)
        for t in range(4):
            pe.matmul(k.db[t][:, 0], k.bones[:], y[:, t], start=True, stop=True).then_inc(mean, 1)
        for t in range(4):
            pe.wait_ge(squared, t + 1)
            pe.matmul(k.db[t][:, 0], k.bones[:], k.sq[t % 2][:], start=True, stop=True).then_inc(var, 1)
            pe.matmul(k.db[t][:, 1], mem.g2[:, t * P:(t + 1) * P], mem.sg[:], start=True, stop=True).then_inc(opened, 1)

    def act(act):
        before(act)
        for t in range(4):
            act.wait_ge(centred, t + 1)
            if t >= 2:
                act.wait_ge(var, t - 1)
            act.activation(k.sq[t % 2][:], y[:, t], ACT.Square).then_inc(squared, 1)
        for t in range(4):
            act.wait_ge(var, t + 1)
            act.activation(mem.rs[t][:], k.db[t][:, 0], ACT.Ln, bias=k.gn_eps[:, 0:1], scale=1.0 / HD).then_inc(root, 1)
        for t in range(4):
            act.wait_ge(root, t + 1)
            act.activation(mem.rs[t][:], mem.rs[t][:], ACT.Exp, scale=-0.5).then_inc(root, 1)
        for t in range(4):
            act.wait_ge(gated, t + 1)
            act.activation(k.x_hi[:, 4 + t], k.ht[t % 2][:], ACT.Copy).then_inc(high, 1)

    def dve(dve):
        before(dve)
        bonus_done(dve)
        for t in range(4):
            dve.wait_ge(mean, t + 1)
            dve.scalar_tensor_tensor(out=y[:, t], in0=k.db[t][:, 0], scalar=-1.0 / HD, in1=y[:, t],
                                     op0=ALU.mult, op1=ALU.add).then_inc(centred, 1)
        for t in range(4):
            dve.wait_ge(root, 5 + t)
            dve.wait_ge(centred, t + 1)
            dve.scalar_tensor_tensor(out=y[:, t], in0=y[:, t], scalar=k.v("ln_g", t), in1=mem.rs[t][:],
                                     op0=ALU.mult, op1=ALU.mult).then_inc(normed, 1)
            dve.wait_ge(normed, t + 1)
            dve.scalar_tensor_tensor(out=y[:, t], in0=y[:, t], scalar=k.v("ln_b", t), in1=mem.bonus[:, t],
                                     op0=ALU.add, op1=ALU.add).then_inc(biased, 1)
            dve.wait_ge(biased, t + 1)
            dve.wait_ge(opened, t + 1)
            if t >= 2:
                dve.wait_ge(low, t - 1)
            dve.tensor_tensor(k.ht[t % 2][:], k.db[t][:, 1], y[:, t], ALU.mult).then_inc(gated, 1)
            dve.wait_ge(high, t + 1)
            dve.tensor_tensor(k.x_lo[:, 4 + t], k.ht[t % 2][:], k.x_hi[:, 4 + t].bitcast(F32), ALU.subtract).then_inc(low, 1)

    phase = Phase(pe=pe, act=act, dve=dve)
    phase.done = lambda eng: (eng.wait_ge(low, 4), eng.wait_ge(high, 4))
    return phase


class Item:

    def __init__(self, q, keys, n, bias, values, out, least=3.0e38):
        self.q, self.keys, self.n, self.bias, self.values, self.out, self.least = q, keys, n, bias, values, out, least


def attention(k, mem, units, finish, before, sem, extra=None, both=True, wait_bias=None, wait_top=None):
    score, low, prob, turned, mixed, taken = (sem(f"at_{n}") for n in ("score", "low", "prob", "turned", "mixed", "taken"))
    copied = [sem(f"at_copied{j}") for j in range(2)]
    items = [(u, it) for u, unit in enumerate(units) for it in unit]
    N = len(items)
    last = {}
    for n, (u, _) in enumerate(items):
        last[u] = n
    score_bank, turn_bank, out_bank = k.ab[0:2], k.ab[2:4], k.gb[0:2]
    per = 2 if extra else 1
    n0, p0, u0 = k.at_items, k.at_exps, k.at_units
    c0 = n0 // 2
    k.at_items, k.at_exps, k.at_units = n0 + N, p0 + N * per, u0 + len(units)

    def pe(pe):
        before(pe)
        for n in range(N + 2):
            if n < N:
                it = items[n][1]
                if n >= 2:
                    pe.wait_ge(low, n0 + n - 1)
                pe.matmul(score_bank[n % 2][:, 0:it.n], it.q, it.keys, start=True, stop=True).then_inc(score, 1)
            m = n - 1
            if 0 <= m < N:
                it = items[m][1]
                pe.wait_ge(prob, p0 + per * (m + 1))
                if m >= 2:
                    pe.wait_ge(copied[m % 2], c0 + m // 2)
                for j, (lo, size, _) in enumerate(it.values):
                    mm = pe.transpose(turn_bank[m % 2][0:size, j * P:(j + 1) * P], mem.pr[m % 2][:, lo:lo + size], k.ident[:])
                mm.then_inc(turned, 1)
            m = n - 2
            if 0 <= m < N:
                u, it = items[m]
                pe.wait_ge(copied[m % 2], c0 + m // 2 + 1)
                if u >= 2:
                    pe.wait_ge(taken, u0 + u - 1)
                for j, (_, size, v) in enumerate(it.values):
                    mm = pe.matmul(out_bank[u % 2][:, it.out], mem.pt[m % 2][0:size, j * P:(j + 1) * P], v,
                                   start=j == 0, stop=j == len(it.values) - 1)
                mm.then_inc(mixed, 1)

    def copy(eng, m):
        it = items[m][1]
        eng.wait_ge(turned, n0 + m + 1)
        if m >= 2:
            eng.wait_ge(mixed, n0 + m - 1)
        size, w = it.values[0][1], len(it.values) * P
        j = m % 2
        if j and both:
            eng.tensor_copy(mem.pt[j][0:size, 0:w], turn_bank[j][0:size, 0:w]).then_inc(copied[j], 1)
        else:
            eng.activation(mem.pt[j][0:size, 0:w], turn_bank[j][0:size, 0:w], ACT.Copy).then_inc(copied[j], 1)

    def act(act):
        before(act)
        for n in range(N + 3):
            if n < N:
                it = items[n][1]
                act.wait_ge(low, n0 + n + 1)
                if n >= 2:
                    act.wait_ge(turned, n0 + n - 1)
                act.activation(mem.pr[n % 2][:, 0:it.n], mem.sc[n % 2][:, 0:it.n], ACT.Exp, bias=mem.mn[:, n:n + 1],
                               scale=-1.0, accum_out=mem.den[:, n:n + 1]).then_inc(prob, 1)
                if extra:
                    extra(act, n, it).then_inc(prob, 1)
            m = n - 3
            if wait_top and 0 <= m < N and last[items[m][0]] == m:
                wait_top(act, items[m][0])
            if 1 <= n <= N and ((n - 1) % 2 == 0 or not both):
                copy(act, n - 1)

    def dve(dve):
        before(dve)
        for n in range(N + 3):
            if n < N:
                it = items[n][1]
                if wait_bias:
                    wait_bias(dve, n)
                dve.wait_ge(score, n0 + n + 1)
                if n >= 2:
                    dve.wait_ge(prob, p0 + per * (n - 1))
                dve.tensor_tensor_reduce(out=mem.sc[n % 2][:, 0:it.n], in0=score_bank[n % 2][:, 0:it.n], in1=it.bias, scale=1.0,
                                         scalar=it.least, op0=ALU.add, op1=ALU.min,
                                         accum_out=mem.mn[:, n:n + 1]).then_inc(low, 1)
            if both and 0 <= n - 1 < N and (n - 1) % 2:
                copy(dve, n - 1)
            m = n - 3
            if 0 <= m < N and last[items[m][0]] == m:
                u = items[m][0]
                dve.wait_ge(mixed, n0 + m + 1)
                finish(dve, u, m, out_bank[u % 2]).then_inc(taken, 1)

    phase = Phase(pe=pe, act=act, dve=dve)
    phase.low, phase.n0 = low, n0
    phase.taken = lambda eng: eng.wait_ge(taken, u0 + len(units))
    return phase


def turn_values(k, pieces, before, sem):
    turned, kept = sem("values_turned"), sem("values_kept")
    n0 = k.values_turned
    k.values_turned += len(pieces)

    def pe(pe):
        before(pe)
        for n, (sources, _) in enumerate(pieces):
            if n >= 4:
                pe.wait_ge(kept, n0 + n - 3)
            for j, s in enumerate(sources):
                mm = pe.transpose(k.ab[n % 4][:, j * P:(j + 1) * P], s, k.ident[:])
            mm.then_inc(turned, 1)

    def act(act):
        before(act)
        for n, (sources, out) in enumerate(pieces):
            act.wait_ge(turned, n0 + n + 1)
            act.activation(out, k.ab[n % 4][:, 0:len(sources) * P], ACT.Copy).then_inc(kept, 1)

    phase = Phase(pe=pe, act=act)
    phase.done = lambda eng: eng.wait_ge(kept, n0 + len(pieces))
    return phase


def swa(k, z, mem, before, sem):
    nb, H = TT, 8
    dsum, rden, bias_done = (sem(f"swa_{n}") for n in ("dsum", "rden", "bias"))
    phases = []
    turn = turn_values(k, [([z[:, 5, t * P:(t + 1) * P] for t in range(4)], mem.vt[:])], before, sem)
    phases.append(turn)

    def biases(dve):
        before(dve)
        dve.wait_ge(mem.loaded2, 16 * 3)
        dve.tensor_scalar(mem.nsink[:], mem.nsink[:], -1.0, None, ALU.mult).then_inc(bias_done, 1)
        for h in range(H):
            slope = 2.0 ** (-8.0 * (h + 1) / H)
            ins = dve.scalar_tensor_tensor(out=mem.bias[:, h], in0=mem.dist[:], scalar=slope, in1=mem.mask[:], op0=ALU.mult, op1=ALU.add)
        ins.then_inc(bias_done, 1)
    phases.append(Phase(dve=biases))

    units = []
    for b in range(nb):
        unit = []
        for h in [x for t in range(4) for x in (t, 4 + t)]:
            grp, t = h // 4, h % 4
            r = slice(grp * HD, (grp + 1) * HD)
            k0 = max(b - 1, 0)
            nk = (b - k0 + 1) * P
            values = [(j * P, P, mem.vt[:, (k0 + j) * P + grp * HD:(k0 + j) * P + (grp + 1) * HD]) for j in range(nk // P)]
            it = Item(z[r, t, b * P:(b + 1) * P], z[r, 4, k0 * P:k0 * P + nk], nk,
                      mem.bias[:, h, 2 * P - nk:2 * P], values, slice(h * HD, (h + 1) * HD), mem.nsink[:, h:h + 1])
            it.h = h
            unit.append(it)
        units.append(unit)

    def ready(eng):
        before(eng)
        turn.done(eng)
        eng.wait_ge(bias_done, 2)

    def extra(act, n, it):
        return act.activation(mem.es[:, n:n + 1], mem.nsink[:, it.h:it.h + 1], ACT.Exp, scale=-1.0, bias=mem.mn[:, n:n + 1])

    def finish(dve, u, m, bank):
        c = slice(8 * u, 8 * u + 8)
        dve.tensor_tensor(mem.den[:, c], mem.den[:, c], mem.es[:, c], ALU.add).then_inc(dsum, 1)
        dve.wait_ge(dsum, u + 1)
        dve.reciprocal(mem.den[:, c], mem.den[:, c]).then_inc(rden, 1)
        dve.wait_ge(rden, u + 1)
        return dve.tensor_tensor(mem.ob[u][:].rearrange("p (g t n) -> p g t n", g=2, t=4),
                                 bank[:].rearrange("p (g t n) -> p g t n", g=2, t=4),
                                 mem.den[:, c].rearrange("p (t g) -> p g t", g=2).unsqueeze(3).to_broadcast([P, 2, 4, HD]), ALU.mult)

    core = attention(k, mem, units, finish, ready, sem, extra)
    phases.append(core)
    out = turn_out(k, mem, 4, 0, core.taken, sem)
    phases.append(out)
    k.phases += phases
    return out.done


def turn_out(k, mem, tiles, first, before, sem):
    turned, high, low = sem("out_turned"), sem("out_high"), sem("out_low")
    n0 = k.outs_turned
    k.outs_turned += tiles

    def pe(pe):
        before(pe)
        for f in range(tiles):
            if f >= 4:
                pe.wait_ge(low, n0 + f - 3)
            for t in range(TT):
                mm = pe.transpose(k.ab[f % 4][:, t * P:(t + 1) * P], mem.ob[t][:, f * P:(f + 1) * P], k.ident[:])
            mm.then_inc(turned, 1)

    def act(act):
        before(act)
        for f in range(tiles):
            act.wait_ge(turned, n0 + f + 1)
            act.activation(k.x_hi[:, first + f], k.ab[f % 4][:], ACT.Copy).then_inc(high, 1)

    def dve(dve):
        before(dve)
        for f in range(tiles):
            dve.wait_ge(high, n0 + f + 1)
            dve.tensor_tensor(k.x_lo[:, first + f], k.ab[f % 4][:], k.x_hi[:, first + f].bitcast(F32),
                              ALU.subtract).then_inc(low, 1)

    phase = Phase(pe=pe, act=act, dve=dve)
    phase.done = lambda eng: eng.wait_ge(low, n0 + tiles)
    return phase


NG, NH = 4, 16
NC = (T - 32) // 16 + 1
CL = 32
ZQ, ZKC, ZVC, ZKS, ZVS, ZKW, ZVW, ZG = 0, 8, 10, 12, 14, 16, 18, 20


def kept_product(k, name, tiles, z, scale, sem):
    g = Product(k, name, tiles, KD, k.x_hi, k.x_lo)
    e = k.input_events

    def act(act):
        k.act_product(act, g, lambda t, i: None)

    def pe(pe):
        pe.wait_ge(k.input_ready, e * KD)
        k.pe_product(pe, g)

    def dve(dve):
        def tile(t, i):
            k.tile_ready(dve, g, t, i)
            out = z[:, t] if isinstance(i, int) else z[:, bass.ds(i * BANKS + t, 1)].rearrange("p o n -> p (o n)")
            dve.tensor_scalar(out, k.gb[g.bank(t)], scale(t + i * BANKS), None, ALU.mult).then_inc(k.bank_free, 1)

        k.sweep(dve, g, tile)

    phase = Phase(sp=lambda sp: k.sp_product(sp, g), act=act, pool=lambda pool: k.pool_product(pool, g), pe=pe, dve=dve)
    phase.g = g
    phase.done = lambda eng: eng.wait_ge(k.bank_free, g.n0 + tiles + BANKS)
    return phase


def nsa_compress(k, z, mem, before, sem):
    windows, hidden, opened, made, kept = (sem(f"cmp_{n}") for n in ("windows", "hidden", "opened", "made", "kept"))
    w1, w2 = (mem.w1k, mem.w1v), (mem.w2k, mem.w2v)

    def dve(dve):
        before(dve)
        for s in range(2):
            dve.wait_ge(mem.loaded_k if s == 0 else mem.loaded_v, 48)
            if s:
                dve.wait_ge(hidden, 1)
            for pair in range(2):
                for a in range(2):
                    src = z[:, (ZVC if s else ZKC) + pair].rearrange("p (c b) -> p b c", b=16)[:, :, a:a + NC]
                    out = mem.win[:, a * 16:(a + 1) * 16, pair * NC:(pair + 1) * NC]
                    pos = (mem.pos_v if s else mem.pos_k)[:, a * 16:(a + 1) * 16].unsqueeze(2).to_broadcast([P, 16, NC])
                    dve.tensor_tensor(out, src, pos, ALU.add).then_inc(windows, 1)

    def pe(pe):
        before(pe)
        for s in range(2):
            pe.wait_ge(windows, 4 * (s + 1))
            for half in range(2):
                r = slice(half * HD, (half + 1) * HD)
                bank = k.gb[half]
                if s:
                    pe.wait_ge(opened, half + 1)
                for ft in range(2):
                    for l in range(CL):
                        mm = pe.matmul(bank[:, ft * 2 * NC:(ft + 1) * 2 * NC], w1[s][r, l * 2 * P + ft * P:l * 2 * P + (ft + 1) * P],
                                       mem.win[r, l], start=l == 0, stop=l == CL - 1)
            mm.then_inc(hidden, 1)
            if s == 0:
                pe.wait_ge(opened, 2)
                for half in range(2):
                    for ft in range(2):
                        mm = pe.matmul(k.ab[0][half * HD:(half + 1) * HD, 0:2 * NC], w2[0][:, ft * HD:(ft + 1) * HD],
                                       mem.hid[:, half, ft * 2 * NC:(ft + 1) * 2 * NC], start=ft == 0, stop=ft == 1)
                mm.then_inc(made, 1)
            else:
                pe.wait_ge(opened, 4)
                for grp in range(NG):
                    pair, half = grp // 2, grp % 2
                    for ft in range(2):
                        c = ft * 2 * NC + pair * NC
                        mm = pe.matmul(k.ab[1][0:NC, grp * HD:(grp + 1) * HD], mem.hid[:, half, c:c + NC],
                                       w2[1][:, ft * HD:(ft + 1) * HD], start=ft == 0, stop=ft == 1)
                mm.then_inc(made, 1)

    def act(act):
        before(act)
        for s in range(2):
            act.wait_ge(hidden, s + 1)
            if s:
                act.wait_ge(made, 1)
            for half in range(2):
                act.activation(mem.hid[:, half], k.gb[half][:, 0:4 * NC], ACT.Gelu_apprx_tanh).then_inc(opened, 1)
        act.wait_ge(made, 1)
        act.activation(mem.kc[:], k.ab[0][:, 0:2 * NC], ACT.Copy).then_inc(kept, 1)
        act.wait_ge(made, 2)
        act.activation(mem.vc[:], k.ab[1][0:NC, 0:NG * HD], ACT.Copy).then_inc(kept, 1)

    phase = Phase(dve=dve, pe=pe, act=act)
    phase.done = lambda eng: eng.wait_ge(kept, 2)
    return phase


def nsa(k, z, mem, before, dram, sem, free_region):
    mem.loaded_k_sem, mem.loaded_v_sem, mem.loaded_b_sem = sem("nsa_loaded_k"), sem("nsa_loaded_v"), sem("nsa_loaded_b")
    mem.loaded_k, mem.loaded_v = mem.loaded_k_sem, mem.loaded_v_sem
    gates_turned, gates_open, valid, bias, inv, coef, prod = (
        sem(f"nsa_{n}") for n in ("gates_turned", "gates_open", "valid", "bias", "inv", "coef", "prod"))

    def load_v(act):
        free_region(act)
        act.dma_start(mem.w1v[:], dram["in_w1v"]).then_inc(mem.loaded_v, 16)
        act.dma_start(mem.w2v[:].rearrange("p (f n) -> p f n", f=2), dram["in_w2v"]).then_inc(mem.loaded_v, 16)
        act.dma_start(mem.pos_v[:], dram["in_pos_v"]).then_inc(mem.loaded_v, 16)
    k.phases.append(Phase(act=load_v))
    comp = nsa_compress(k, z, mem, before, sem)
    k.phases.append(comp)

    def load_tables(act):
        comp.done(act)
        act.dma_start(mem.dist[:], dram["c_nsa_dist"]).then_inc(mem.loaded_b_sem, 16)
        act.dma_start(mem.mask[:], dram["c_nsa_mask"]).then_inc(mem.loaded_b_sem, 16)
    k.phases.append(Phase(act=load_tables))
    turn = turn_values(k, [([z[:, v + j, t * P:(t + 1) * P] for v in (ZVS, ZVW) for j in range(2)], mem.vt[t][:]) for t in range(TT)],
                       comp.done, sem)
    k.phases.append(turn)

    def gates_pe(pe):
        comp.done(pe)
        for t in range(TT):
            mm = pe.transpose(k.gb[3][:, t * P:(t + 1) * P], z[:, ZG, t * P:(t + 1) * P], k.ident[:])
        mm.then_inc(gates_turned, 1)

    def gates_act(act):
        act.wait_ge(gates_turned, 1)
        act.activation(mem.gates[:], k.gb[3][:].rearrange("p (t n) -> p t n", t=TT)[:, :, 0:3 * NH], ACT.Sigmoid).then_inc(gates_open, 1)

    def gates_dve(dve):
        dve.wait_ge(gates_open, 1)
        g0 = mem.gates[:, 0].rearrange("p (h b) -> p h b", b=3)[:, :, 0]
        dve.tensor_scalar(g0, g0, k.first_block[:, 0:1], None, ALU.mult).then_inc(valid, 1)
    k.phases.append(Phase(pe=gates_pe, act=gates_act, dve=gates_dve))

    units, heads = [], []
    for h in range(NH):
        grp = h // 4
        half, pair = grp % 2, grp // 2
        r = slice(half * HD, (half + 1) * HD)
        b = mem.bias[h % 2]
        for t in range(TT):
            q = z[r, ZQ + pair * 4 + h % 4, t * P:(t + 1) * P]
            w0 = max(t - 2, 0)
            nw = (t - w0 + 1) * P
            ns = (t + 1) * P

            def values(first, n, v):
                return [(j * P, P, mem.vt[first + j][:, (v * NG + grp) * HD:(v * NG + grp + 1) * HD]) for j in range(n // P)]
            units.append([
                Item(q, mem.kc[r, pair * NC:(pair + 1) * NC], NC, b[:, 7 * P + t * NC:7 * P + (t + 1) * NC],
                     [(0, NC, mem.vc[:, grp * HD:(grp + 1) * HD])], slice(0, HD)),
                Item(q, z[r, ZKS + pair, 0:ns], ns, b[:, 4 * P - ns:4 * P], values(0, ns, 0), slice(HD, 2 * HD)),
                Item(q, z[r, ZKW + pair, w0 * P:w0 * P + nw], nw, b[:, 7 * P - nw:7 * P], values(w0, nw, 1), slice(2 * HD, 3 * HD)),
            ])
            heads.append((h, t))

    def ready(eng):
        turn.done(eng)
        eng.wait_ge(valid, 1)

    def finish(dve, u, m, bank):
        h, t = heads[u]
        c = slice(3 * u, 3 * u + 3)
        dve.reciprocal(mem.den[:, c], mem.den[:, c]).then_inc(inv, 1)
        dve.wait_ge(inv, u + 1)
        dve.tensor_tensor(mem.den[:, c], mem.den[:, c], mem.gates[:, t, 3 * h:3 * h + 3], ALU.mult).then_inc(coef, 1)
        dve.wait_ge(coef, u + 1)
        dve.tensor_tensor(mem.prod[:].rearrange("p (b n) -> p b n", b=3), bank[:, 0:3 * HD].rearrange("p (b n) -> p b n", b=3),
                          mem.den[:, c].unsqueeze(2).to_broadcast([P, 3, HD]), ALU.mult).then_inc(prod, 1)
        dve.wait_ge(prod, u + 1)
        return dve.tensor_reduce(mem.ob[t][:, h * HD:(h + 1) * HD], mem.prod[:].rearrange("p (b n) -> p n b", b=3), AX.X, ALU.add)

    core = attention(k, mem, units, finish, ready, sem, both=False, wait_bias=lambda dve, n: dve.wait_ge(bias, 2 * (n // 12) + 2))

    def biases(pool):
        pool.wait_ge(mem.loaded_b_sem, 32)
        for h in range(NH):
            if h >= 2:
                pool.wait_ge(core.low, core.n0 + 12 * (h - 1))
            slope = 2.0 ** (-8.0 * (h + 1) / NH)
            b = mem.bias[h % 2]
            pool.tensor_scalar(b[:], mem.dist[:], slope, 1.0, ALU.mult, ALU.mult).then_inc(bias, 1)
            pool.wait_ge(bias, 2 * h + 1)
            pool.tensor_tensor(b[:], b[:], mem.mask[:], ALU.add).then_inc(bias, 1)
    core.pool = biases
    k.phases.append(core)
    out = turn_out(k, mem, KD, 0, core.taken, sem)
    k.phases.append(out)
    return out.done


SLOTS_H, GROUPS = 4, 3
LRU_TAPS = 4


def lru_input(k, name, mem, sem):
    g = Product(k, name, KD, KD, k.x_hi, k.x_lo)
    e = k.input_events
    first, tap1, tap2 = (sem(f"lru_{n}") for n in ("first", "tap1", "tap2"))

    def col(t, i, lo=0):
        return mem.xc[:, t, lo:T] if isinstance(i, int) else mem.xc[:, bass.ds(i * BANKS + t, 1), lo:T].rearrange("p o n -> p (o n)")

    def act(act):
        def tile(t, i):
            k.tile_ready(act, g, t, i)
            act.activation(col(t, i), k.gb[g.bank(t)], ACT.Identity, bias=k.v("lconv_b", t + i * BANKS),
                           scale=k.v("lconv_w3", t + i * BANKS)).then_inc(first, 1)
        k.act_product(act, g, tile)

    def pe(pe):
        pe.wait_ge(k.input_ready, e * KD)
        k.pe_product(pe, g)

    def dve(dve):
        def tile(t, i):
            for d, (before, after) in enumerate(((first, tap1), (tap1, tap2), (tap2, k.bank_free)), 1):
                dve.wait_ge(before, t + 1 + i * BANKS)
                dve.scalar_tensor_tensor(out=col(t, i, d), in0=k.gb[g.bank(t)][:, 0:T - d], scalar=k.v(f"lconv_w{3 - d}", t + i * BANKS),
                                         in1=col(t, i, d), op0=ALU.mult, op1=ALU.add).then_inc(after, 1)
        k.sweep(dve, g, tile)

    phase = Phase(sp=lambda sp: k.sp_product(sp, g), act=act, pool=lambda pool: k.pool_product(pool, g), pe=pe, dve=dve)
    phase.g = g
    phase.done = lambda eng: eng.wait_ge(k.bank_free, g.n0 + KD + BANKS)
    return phase


def lru_scan(k, mem, before, sem):
    pair, gx, ga, ex, th, m1, q, a, root, b, bb, h, sp = (
        sem(f"lru_{n}") for n in ("pair", "gx", "ga", "ex", "th", "m1", "q", "a", "root", "b", "bb", "h", "sp"))
    c = mem.lru_small

    def pe(pe):
        before(pe)
        pe.wait_ge(mem.loaded, 32)
        for t in range(KD):
            head, nt = t // 2, t % 2
            if t >= 4:
                pe.wait_ge(ga, t - 3)
            for bank, w in ((k.db[t % 4][:, 0], mem.wx), (k.db[t % 4][:, 1], mem.wa)):
                for kt in range(2):
                    o = ((head * 2 + kt) * 2 + nt) * P
                    mm = pe.matmul(bank, w[:, o:o + P], mem.xc[:, head * 2 + kt], start=kt == 0, stop=kt == 1)
            mm.then_inc(pair, 1)
        pe.wait_ge(ga, KD)

    def act(act):
        before(act)
        act.activation(c[:, 0], k.v("a_param", 0, KD), ACT.Abs).then_inc(sp, 1)
        act.wait_ge(sp, 1)
        act.activation(c[:, 0], c[:, 0], ACT.Exp, scale=-1.0).then_inc(sp, 1)
        act.wait_ge(sp, 2)
        act.activation(c[:, 0], c[:, 0], ACT.Ln, bias=k.ones[:, 0:1]).then_inc(sp, 1)
        for t in range(KD):
            act.wait_ge(pair, t + 1)
            act.activation(mem.gx[:, t], k.db[t % 4][:, 0], ACT.Sigmoid, bias=k.v("b_x", t)).then_inc(gx, 1)
            act.activation(mem.ga[:, t], k.db[t % 4][:, 1], ACT.Sigmoid, bias=k.v("b_a", t)).then_inc(ga, 1)
        act.wait_ge(sp, 7)
        for t in range(KD):
            act.wait_ge(ga, t + 1)
            act.activation(mem.e[:, t], mem.ga[:, t], ACT.Exp, scale=c[:, 2, t:t + 1]).then_inc(ex, 1)
            act.activation(mem.ga[:, t], mem.ga[:, t], ACT.Tanh, scale=c[:, 3, t:t + 1]).then_inc(th, 1)
        for t in range(KD):
            act.wait_ge(q, t + 1)
            act.activation(mem.ga[:, t], mem.ga[:, t], ACT.Sqrt, scale=-1.0).then_inc(root, 1)

    def dve(dve):
        before(dve)
        dve.wait_ge(sp, 3)
        dve.tensor_scalar(c[:, 1], k.v("a_param", 0, KD), -1.0, 0.0, ALU.mult, ALU.max).then_inc(sp, 1)
        dve.wait_ge(sp, 4)
        dve.tensor_tensor(c[:, 1], c[:, 1], c[:, 0], ALU.add).then_inc(sp, 1)
        dve.wait_ge(sp, 5)
        dve.tensor_scalar(c[:, 2], c[:, 1], -8.0, None, ALU.mult).then_inc(sp, 1)
        dve.tensor_scalar(c[:, 3], c[:, 1], -4.0, None, ALU.mult).then_inc(sp, 1)
        for t in range(KD):
            dve.wait_ge(th, t + 1)
            dve.scalar_tensor_tensor(out=mem.e[:, t], in0=mem.e[:, t], scalar=1.0, in1=mem.ga[:, t],
                                     op0=ALU.add, op1=ALU.mult).then_inc(m1, 1)
            dve.wait_ge(m1, t + 1)
            dve.scalar_tensor_tensor(out=mem.ga[:, t], in0=mem.e[:, t], scalar=2.0, in1=mem.e[:, t],
                                     op0=ALU.add, op1=ALU.mult).then_inc(q, 1)
            dve.wait_ge(q, t + 1)
            dve.tensor_scalar(mem.e[:, t], mem.e[:, t], 1.0, None, ALU.add).then_inc(a, 1)
            dve.tensor_tensor(mem.gx[:, t], mem.gx[:, t], mem.xc[:, t], ALU.mult).then_inc(b, 1)
        for t in range(KD):
            dve.wait_ge(root, t + 1)
            dve.wait_ge(b, t + 1)
            dve.tensor_tensor(mem.gx[:, t], mem.gx[:, t], mem.ga[:, t], ALU.mult).then_inc(bb, 1)
            dve.wait_ge(bb, t + 1)
            dve.wait_ge(a, t + 1)
            dve.tensor_tensor_scan(mem.h[:, t], mem.e[:, t], mem.gx[:, t], 0.0, ALU.mult, ALU.add).then_inc(h, 1)

    phase = Phase(pe=pe, act=act, dve=dve)
    phase.done = lambda eng: eng.wait_ge(h, KD)
    phase.dve_done = phase.done
    return phase


def lru_gate(k, name, mem, scanned, sem):
    g = Product(k, name, KD, KD, k.x_hi, k.x_lo)
    opened, product, high, low = (sem(f"rec_{n}") for n in ("opened", "product", "high", "low"))

    def col(f, t, i):
        return f[:, t] if isinstance(i, int) else f[:, bass.ds(i * BANKS + t, 1)].rearrange("p o n -> p (o n)")

    def act(act):
        scanned(act)

        def tile(t, i):
            k.tile_ready(act, g, t, i)
            act.wait_ge(product, t + 1 + i * BANKS)
            act.activation(mem.c[t % 2][:], k.gb[g.bank(t)], ACT.Gelu_apprx_tanh).then_inc(opened, 1)
            act.wait_ge(product, t + 3 + i * BANKS)
            act.activation(col(mem.rec_hi, t, i), k.ht[t % 2][:], ACT.Copy).then_inc(high, 1)
        k.act_product(act, g, tile)

    def dve(dve):
        scanned(dve)
        dve.sem_inc(product, 2)

        def tile(t, i):
            dve.wait_ge(opened, t + 1 + i * BANKS)
            dve.sem_inc(k.bank_free, 1)
            dve.tensor_tensor(k.ht[t % 2][:], mem.c[t % 2][:], col(mem.h, t, i), ALU.mult).then_inc(product, 1)
            dve.wait_ge(high, t + 1 + i * BANKS)
            dve.tensor_tensor(col(mem.rec_lo, t, i), k.ht[t % 2][:], col(mem.rec_hi, t, i).bitcast(F32), ALU.subtract).then_inc(low, 1)
        k.sweep(dve, g, tile)

    phase = Phase(sp=lambda sp: k.sp_product(sp, g), act=act, pool=lambda pool: k.pool_product(pool, g),
                  pe=lambda pe: k.pe_product(pe, g), dve=dve)
    phase.g = g
    phase.done = lambda eng: eng.wait_ge(low, KD)
    return phase


def bias_vectors(k, mem, dram, sem):
    picked, made, written = sem("rel_picked"), sem("rel_made"), sem("rel_written")
    n = mem.pick.shape[1]
    half = n // 2

    def pe(pe):
        pe.wait_ge(mem.loaded_rel, 48)
        for j in range(2):
            mm = pe.matmul(k.ab[2 + j][0:12, 0:half], mem.table[:], mem.pick[:, j * half:(j + 1) * half], start=True, stop=True)
        mm.then_inc(picked, 1)

    def dve(dve):
        dve.wait_ge(picked, 1)
        for j in range(2):
            dve.tensor_tensor(mem.rv[:, j * half:(j + 1) * half], mem.rmask[:, j * half:(j + 1) * half], k.ab[2 + j][0:12, 0:half],
                              ALU.subtract).then_inc(made, 1)

    def act(act):
        act.wait_ge(made, 2)
        act.dma_start(dram["rv"], mem.rv[:]).then_inc(written, 16)
    phase = Phase(pe=pe, dve=dve, act=act)
    phase.written = lambda eng: eng.wait_ge(written, 16)
    return phase


def dilated(k, mem, s, before, dram, rv_written, sem):
    tag = "dil"
    loaded, flipped, ordered, coef, prod, far, top, c, dd = (
        sem(f"{tag}_{n}") for n in ("loaded", "flipped", "ordered", "coef", "prod", "far", "top", "c", "dd"))

    def load(act):
        before(act)
        rv_written(act)
        for g in range(GROUPS):
            row = dram["rv"][g * SLOTS_H + s]
            src = bass.AP(tensor=row.tensor, offset=row.offset, ap=[[1, P], [1, T]])
            act.dma_start(mem.bias[g][:], src).then_inc(loaded, 16)

    def flip(pe):
        pe.wait_ge(loaded, 16 * GROUPS * (s + 1))
        before(pe)
        for g in range(GROUPS):
            pe.matmul(k.ab[g], k.flip, mem.bias[g][:], start=True, stop=True).then_inc(flipped, 1)

    def keep(dve):
        before(dve)
        for g in range(GROUPS):
            dve.wait_ge(flipped, GROUPS * s + g + 1)
            dve.tensor_copy(mem.bias[g][:], k.ab[g]).then_inc(ordered, 1)
    k.phases.append(Phase(act=load, pe=flip, dve=keep))
    turn = turn_values(k, [([mem.z[:, 3 * g + 2, t * P:(t + 1) * P] for t in range(TT)], mem.vt[g][:]) for g in range(GROUPS)],
                       lambda eng: (before(eng), eng.wait_ge(ordered, GROUPS * (s + 1))), sem)
    k.phases.append(turn)
    units = []
    for t in range(TT):
        unit = []
        for g in range(GROUPS):
            k0 = max(t - 1, 0) if g == 0 else 0
            n = (t - k0 + 1) * P
            unit.append(Item(mem.z[:, 3 * g, t * P:(t + 1) * P], mem.z[:, 3 * g + 1, k0 * P:k0 * P + n], n, mem.bias[g][:, T - n:T],
                             [(j * P, P, mem.vt[g][:, (k0 + j) * P:(k0 + j + 1) * P]) for j in range(n // P)],
                             slice(g * P, (g + 1) * P)))
        units.append(unit)

    def finish(dve, u, m, bank):
        x = slice(3 * u, 3 * u + 3)
        n = TT * s + u
        v = mem.sm
        dve.tensor_reduce(v[:, 0:1], mem.mn[:, x], AX.X, ALU.min).then_inc(far, 1)
        dve.wait_ge(far, n + 1)
        dve.tensor_scalar(v[:, 1:4], mem.mn[:, x], v[:, 0:1], None, ALU.subtract).then_inc(top, 1)
        dve.wait_ge(c, n + 1)
        dve.tensor_tensor(v[:, 8:11], v[:, 4:7], mem.den[:, x], ALU.mult).then_inc(dd, 1)
        dve.wait_ge(dd, 3 * n + 1)
        dve.tensor_reduce(v[:, 11:12], v[:, 8:11], AX.X, ALU.add).then_inc(dd, 1)
        dve.wait_ge(dd, 3 * n + 2)
        dve.reciprocal(v[:, 12:13], v[:, 11:12]).then_inc(dd, 1)
        dve.wait_ge(dd, 3 * n + 3)
        dve.tensor_scalar(v[:, 13:16], v[:, 4:7], v[:, 12:13], None, ALU.mult).then_inc(coef, 1)
        dve.wait_ge(coef, n + 1)
        dve.tensor_tensor(mem.prod[:].rearrange("p (b n) -> p b n", b=3), bank[:, 0:3 * P].rearrange("p (b n) -> p b n", b=3),
                          v[:, 13:16].unsqueeze(2).to_broadcast([P, 3, P]), ALU.mult).then_inc(prod, 1)
        dve.wait_ge(prod, n + 1)
        return dve.tensor_reduce(mem.ob[u][:], mem.prod[:].rearrange("p (b n) -> p n b", b=3), AX.X, ALU.add)

    def ready(eng):
        turn.done(eng)
        eng.wait_ge(ordered, GROUPS * (s + 1))

    core = attention(k, mem, units, finish, ready, sem, wait_top=lambda act, u: (
        act.wait_ge(top, TT * s + u + 1),
        act.activation(mem.sm[:, 4:7], mem.sm[:, 1:4], ACT.Exp, scale=-1.0).then_inc(c, 1)))
    k.phases.append(core)

    turned, high, low = sem("out_turned"), sem("out_high"), sem("out_low")
    n0 = k.outs_turned
    k.outs_turned += 1

    def pe(pe):
        core.taken(pe)
        for t in range(TT):
            mm = pe.transpose(k.ab[3][:, t * P:(t + 1) * P], mem.ob[t][:], k.ident[:])
        mm.then_inc(turned, 1)

    def act(act):
        act.wait_ge(turned, n0 + 1)
        act.activation(mem.at_hi[:, s], k.ab[3], ACT.Copy).then_inc(high, 1)

    def dve(dve):
        dve.wait_ge(high, n0 + 1)
        dve.tensor_tensor(mem.at_lo[:, s], k.ab[3], mem.at_hi[:, s].bitcast(F32), ALU.subtract).then_inc(low, 1)
    k.phases.append(Phase(pe=pe, act=act, dve=dve))
    return lambda eng: eng.wait_ge(low, n0 + 1)


class Blend(Product):

    def __init__(self, k, names, inputs):
        self.upt, self.tiles, self.units = 1, 4 * KD, 4 * KD
        self.parts = [(w.shape[2] // P, *x) for w, x in zip([k.w[n] for n in names], inputs)]
        self.ws = [k.w[n] for n in names]
        self.u0, self.n0 = k.units, k.tiles
        k.units += self.units
        k.tiles += self.tiles
        k.nb += [p[0] for p in self.parts] * KD
        self.loops, self.rest = KD, 0

    def part(self, t):
        return self.parts[t % 4]

    def source(self, j, i, step):
        w = self.ws[j % 4]
        return w[j // 4] if isinstance(i, int) else w[bass.ds(i, 1)].rearrange("o p n -> (o p) n")


def blend(k, names, inputs, mem, ready, sem):
    g = Blend(k, names, inputs)
    opened, product, summed, high, low = (sem(f"bl_{n}") for n in ("opened", "product", "summed", "high", "low"))

    def col(f, i):
        return f[:, i] if isinstance(i, int) else f[:, bass.ds(i, 1)].rearrange("p o n -> p (o n)")

    def act(act):
        def tile(t, i):
            b, f = t % 4, t // 4 + i
            if b % 2:
                k.tile_ready(act, g, t, i)
                act.wait_ge(product, (b // 2) + 1 + 2 * f)
                act.activation(mem.c[b // 2][:], k.gb[g.bank(t)], ACT.Sigmoid).then_inc(opened, 1)
            if b == 3:
                act.wait_ge(summed, f + 1)
                act.activation(col(mem.m_hi, f), k.r[:], ACT.Copy).then_inc(high, 1)
        k.act_product(act, g, tile)

    def pe(pe):
        ready(pe)
        k.pe_product(pe, g)

    def dve(dve):
        dve.sem_inc(product, 2)

        def tile(t, i):
            b, f = t % 4, t // 4 + i
            if b % 2:
                dve.wait_ge(opened, (b // 2) + 1 + 2 * f)
                dve.tensor_tensor(k.ht[b // 2][:], mem.c[b // 2][:], k.gb[g.bank(t - 1)], ALU.mult).then_inc(product, 1)
                dve.wait_ge(product, (b // 2) + 3 + 2 * f)
                dve.sem_inc(k.bank_free, 2)
            if b == 3:
                dve.wait_ge(low, f + 1)
                dve.tensor_tensor(k.r[:], k.ht[0][:], k.ht[1][:], ALU.add).then_inc(summed, 1)
                dve.wait_ge(high, f + 1)
                dve.tensor_tensor(col(mem.m_lo, f), k.r[:], col(mem.m_hi, f).bitcast(F32), ALU.subtract).then_inc(low, 1)
        dve.sem_inc(low, 1)
        k.sweep(dve, g, tile)

    phase = Phase(sp=lambda sp: k.sp_product(sp, g), act=act, pool=lambda pool: k.pool_product(pool, g), pe=pe, dve=dve)
    phase.g = g
    phase.done = lambda eng: eng.wait_ge(low, KD + 1)
    return phase


class Memory:
    pass


def shape_constants():
    p, n = np.arange(P)[:, None], np.arange(P)[None, :]
    chunk, block = p // CH == n // CH, p // 16 == n // 16
    c = {
        "ident": p == n,
        "bones": p // HD == n // HD,
        "d": (n < p) & block,
        "lo": (n < p) & chunk & ~block,
        "dt": (p < n) & block,
        "upper": (p < n) & chunk,
        "upto": (p <= n) & chunk,
        "flip": p + n == P - 1,
        "eye2": p % HD == np.arange(HD)[None, :],
    }
    own = {"keep": np.broadcast_to((np.arange(T) % CH != 0)[None], (P, T))}
    dist = p + P - np.arange(2 * P)[None]
    own["swa_dist"] = dist
    own["swa_mask"] = np.where((dist < 0) | (dist >= 128), BIG, 0.0)
    sel = p + 3 * P - np.arange(4 * P)[None]
    win = p + 2 * P - np.arange(3 * P)[None]
    cmp_ = np.concatenate([p + t * P - (16 * np.arange(NC)[None] + CL - 1) for t in range(TT)], 1)
    dist = np.concatenate([sel, win, cmp_], 1)
    own["nsa_dist"] = dist
    far = np.concatenate([sel < 0, (win < 0) | (win >= 256), cmp_ < 0], 1)
    own["nsa_mask"] = np.where(far, BIG, 0.0)
    back = T - 1 - np.arange(T + P)
    far, near = np.float32(2048 / 16), np.maximum(back, 1).astype(np.float32)
    bucket = np.where(back < 16, np.maximum(back, 0), np.minimum(16 + (np.log(near / np.float32(16)) / np.log(far) * 16).astype(np.int32), 31))
    own["pick"] = np.arange(32)[:, None] == bucket[None]
    own["rmask"] = np.repeat(np.stack([np.where((back < 0) | (back % d != 0) | (back > 128 * d), BIG, 0.0) for d in (1, 4, 16)]), 4, 0)
    c["first_block"] = p >= CL - 1
    f = lambda d: {n: np.ascontiguousarray(v, dtype=np.float32) for n, v in d.items()}
    return f(c), f(own)


def build(nc, dram, cols, ccols, out):
    names = {}
    with ExitStack() as ctx:
        def sem(name):
            if name not in names:
                names[name] = ctx.enter_context(nc.semaphore(name))
            return names[name]

        def sb(name, shape, dt=F32, stack=ctx):
            return stack.enter_context(nc.sbuf_tensor(name, shape, dt))

        w = {n[2:]: v for n, v in dram.items() if n.startswith("w_")}
        vec = sb("vec", [P, dram["in_vec"].shape[1]])
        const = sb("const", [P, dram["in_const"].shape[1]])
        k = Kit(nc, w, vec, cols)

        def cc(name, n=P):
            return const[:, ccols[name]:ccols[name] + n]

        k.first_block = cc("first_block", 1)
        k.ident, k.bones, k.eye2 = cc("ident"), cc("bones"), cc("eye2", HD)
        k.flip = cc("flip")
        k.mask = {n: cc(n) for n in ("d", "lo", "dt", "upper", "upto")}
        k.x = sb("x_res", [P, KD, T])
        k.raw = [sb(f"raw{j}", [P, NBMAX * P]) for j in range(SLOTS)]
        k.w_hi = [sb(f"w_hi{j}", [P, NBMAX * P], F32R) for j in range(PAIRS)]
        k.w_lo = [sb(f"w_lo{j}", [P, NBMAX * P], F32R) for j in range(PAIRS)]
        k.sq = [sb(f"sq{j}", [P, T]) for j in range(2)]
        k.ht = [sb(f"ht{j}", [P, T]) for j in range(2)]
        k.acc, k.ln, k.r = sb("acc", [P, T]), sb("ln", [P, T]), sb("r", [P, T])
        k.ones, k.eps, k.gn_eps, k.keep_scale = sb("ones", [P, P]), sb("eps", [P, 1]), sb("gn_eps", [P, 1]), sb("keep_scale", [P, 20])
        psum = ctx.enter_context(nc.psum_tensor("psum", [P, 8, T], F32))
        k.gb = [psum[:, j] for j in range(4)]
        k.ab = [psum[:, 4 + j] for j in range(4)]
        k.db = [psum[:, 2 * j:2 * j + 2] for j in range(4)]
        k.raw_in = [sem(f"raw_in{j}") for j in range(SLOTS)]
        k.hi_done, k.lo_done, k.mm, k.bank_free = sem("hi_done"), sem("lo_done"), sem("mm"), sem("bank_free")
        k.input_ready, k.x_updated = sem("input_ready"), sem("x_updated")
        loaded, set_up, stored = sem("loaded"), sem("set_up"), sem("stored")

        ffn, L0 = Memory(), Memory()
        with ExitStack() as s:
            ffn.m = sb("ffn_m", [P, KD, T], stack=s)
        with ExitStack() as s:
            L0.d, L0.dt, L0.lo, L0.d2, L0.d2t, L0.i1, L0.i2, L0.ak = (
                sb(f"rw_{n}", [P, D], stack=s) for n in ("d", "dt", "lo", "d2", "d2t", "i1", "i2", "ak"))
        with ExitStack() as s:
            w1v = sb("nsa_w1v", [P, CL * 2 * P], stack=s)
        with ExitStack() as s:
            L0.wa2 = sb("rw_wa2", [P, T], stack=s)
        k.x_hi = sb("x_hi", [P, KD, T], F32R)
        k.x_lo = sb("x_lo", [P, KD, T], F32R)
        with ExitStack() as s:
            ffn.h_hi = sb("h_hi", [P, KF, T], F32R, s)
            ffn.h_lo = sb("h_lo", [P, KF, T], F32R, s)
            ffn.c = [sb(f"ffn_c{j}", [P, T], stack=s) for j in range(2)]
        S = Memory()
        with ExitStack() as s:
            z0 = sb("z0", [P, 20, T], stack=s)
            L0.a, L0.b, L0.bonus = (sb(f"rw_{n}", [P, 4, T], stack=s) for n in ("a", "b", "bonus"))
            L0.sg, L0.pc = sb("rw_sg", [P, T], stack=s), sb("rw_pc", [P, 4, 2 * TT], stack=s)
            with ExitStack() as s2:
                L0.ld, L0.l, L0.e1 = (sb(f"rw_{n}", [P, 4, T], stack=s2) for n in ("ld", "l", "e1"))
                L0.keep = sb("rw_keep", [P, T], stack=s2)
            with ExitStack() as s2:
                L0.x0, L0.x1, L0.tv_bd, L0.b_bd, L0.v_bd, L0.gt = (
                    sb(f"rw_{n}", [P, D], stack=s2) for n in ("x0", "x1", "tv_bd", "b_bd", "v_bd", "gt"))
                L0.vt, L0.bt = (sb(f"rw_{n}", [P, T], stack=s2) for n in ("vt", "bt"))
            with ExitStack() as s2:
                L0.rs = [sb(f"rw_rs{j}", [P, T], stack=s2) for j in range(4)]
                L0.g2 = sb("rw_g2", [P, T], stack=s2)
        with ExitStack() as s:
            sb("z0_again", [P, 20, T], stack=s)
            S.vt = sb("swa_vt", [P, T], stack=s)
            S.bias = sb("swa_bias", [P, 8, 2 * P], stack=s)
            S.ob = [sb(f"swa_ob{j}", [P, T], stack=s) for j in range(TT)]
            S.sc, S.pr, S.pt = ([sb(f"swa_{n}{j}", [P, 2 * P], stack=s) for j in range(2)] for n in ("sc", "pr", "pt"))
            S.dist, S.mask, S.nsink = sb("swa_dist", [P, 2 * P], stack=s), sb("swa_mask", [P, 2 * P], stack=s), sb("swa_nsink", [P, 8], stack=s)
            S.mn, S.den, S.es = (sb(f"swa_{n}", [P, 32], stack=s) for n in ("mn", "den", "es"))
        with ExitStack() as s:
            mix_m = sb("mix_m", [P, KD, T], stack=s)
        B = Memory()
        with ExitStack() as s:
            B.rec_hi, B.rec_lo = sb("rec_hi", [P, KD, T], F32R, s), sb("rec_lo", [P, KD, T], F32R, s)
            with ExitStack() as s2:
                sb("lru_gx_region", [P, KD, T], stack=s2)
                B.e = sb("lru_e", [P, KD, T], stack=s2)
                B.ga = sb("lru_ga", [P, KD, T], stack=s2)
                B.lru_small = sb("lru_small", [P, 4, KD], stack=s2)
            with ExitStack() as s2:
                B.pick, B.rmask, B.rv, B.table = (sb(f"rel_{n}", shape, stack=s2) for n, shape in (
                    ("pick", [32, T + P]), ("mask", [12, T + P]), ("rv", [12, T + P]), ("table", [32, 12])))
            with ExitStack() as s2:
                B.gx = sb("lru_gx", [P, KD, T], stack=s2)
            B.h = B.ga
            with ExitStack() as s2:
                B.at_hi, B.at_lo = sb("at_hi", [P, 4, T], F32R, s2), sb("at_lo", [P, 4, T], F32R, s2)
                with ExitStack() as s3:
                    B.z = sb("z2", [P, 9, T], stack=s3)
                    B.vt = [sb(f"dil_vt{g}", [P, T], stack=s3) for g in range(3)]
                    B.bias = [sb(f"dil_bias{g}", [P, T], stack=s3) for g in range(3)]
                    B.ob = [sb(f"dil_ob{t}", [P, P], stack=s3) for t in range(TT)]
                    B.mn, B.den, B.prod, B.sm = sb("dil_mn", [P, 12], stack=s3), sb("dil_den", [P, 12], stack=s3), sb("dil_prod", [P, 3 * P], stack=s3), sb("dil_small", [P, 16], stack=s3)
                    B.end = sb("dil_end", [P, 1], stack=s3)
                with ExitStack() as s3:
                    B.m_hi, B.m_lo = sb("m_hi", [P, KD, T], F32R, s3), sb("m_lo", [P, KD, T], F32R, s3)
        with ExitStack() as s:
            B.xc = sb("lru_xc", [P, KD, T], stack=s)
            B.wx, B.wa = sb("lru_wx", [P, 2 * D], stack=s), sb("lru_wa", [P, 2 * D], stack=s)
        B.sc, B.pr, B.pt = k.sq, k.ht, [k.acc, k.ln]
        B.c = k.sq
        N = Memory()
        with ExitStack() as s:
            z1 = sb("z1", [P, 21, T], stack=s)
            N.gates, N.kc, N.vc = sb("nsa_gates", [P, TT, 3 * NH], stack=s), sb("nsa_kc", [P, 2 * NC], stack=s), sb("nsa_vc", [NC, NG * HD], stack=s)
            N.mn, N.den, N.prod = sb("nsa_mn", [P, 192], stack=s), sb("nsa_den", [P, 192], stack=s), sb("nsa_prod", [P, 3 * HD], stack=s)
            with ExitStack() as s2:
                N.vt = [sb(f"nsa_vt{t}", [P, T], stack=s2) for t in range(TT)]
                N.ob = [sb(f"nsa_ob{t}", [P, D], stack=s2) for t in range(TT)]
                nb = 7 * P + TT * NC
                N.bias = [sb(f"nsa_bias{j}", [P, nb], stack=s2) for j in range(2)]
                N.dist, N.mask = sb("nsa_dist", [P, nb], stack=s2), sb("nsa_mask", [P, nb], stack=s2)
            with ExitStack() as s2:
                N.w1k = sb("nsa_w1k", [P, CL * 2 * P], stack=s2)
                N.win = sb("nsa_win", [P, CL, 2 * NC], stack=s2)
                N.hid = sb("nsa_hid", [P, 2, 4 * NC], stack=s2)
                N.w2k, N.w2v = sb("nsa_w2k", [P, P], stack=s2), sb("nsa_w2v", [P, P], stack=s2)
                N.pos_k, N.pos_v = sb("nsa_pos_k", [P, CL], stack=s2), sb("nsa_pos_v", [P, CL], stack=s2)
        N.sc, N.pr, N.pt = k.sq, k.ht, [k.acc, k.ln]
        L0.y, L0.kt, L0.h, L0.rq, L0.y2, L0.s_bd, L0.tmp = L0.a, k.r, k.sq[0], k.sq[1], k.ht[0], k.ht[1], k.ln
        L0.s = [k.acc[:, 0:4 * HD], k.acc[:, 4 * HD:8 * HD]]

        free = PAIRS
        wait_x = lambda eng, t: eng.wait_ge(loaded, 16 * 3)

        def updated():
            e = k.update_events - 1
            return lambda eng, t: eng.wait_ge(k.x_updated, e * KD + t + 1)

        k.phases.append(pre_norm(k, "mix_pre0", sem, wait_x, free))
        hy_in = shifted_product(k, "hy_in", 20, z0, lambda t: k.keep_scale[:, bass.ds(t, 1)] if not isinstance(t, int) else k.keep_scale[:, t:t + 1],
                                lambda t: k.v("mu", t), sem)
        k.phases.append(hy_in)
        z_ready = lambda eng: eng.wait_ge(k.bank_free, hy_in.g.n0 + 20 + BANKS)
        L0.loaded, L0.late, L0.n_loads, S.loaded2 = sem("rw_loaded"), sem("rw_late"), 2, sem("swa_loaded")

        def load_rwkv(act):
            act.wait_ge(k.mm, hy_in.g.end())
            act.dma_start(L0.wa2[:], dram["in_wa2"]).then_inc(L0.loaded, 16)
            act.dma_start(L0.keep[:], dram["c_keep"]).then_inc(L0.loaded, 16)
        k.phases.append(Phase(act=load_rwkv))
        prelude = rwkv_prelude(k, z0, L0, z_ready, sem)
        k.phases.append(prelude)
        cleared = sem("rw_cleared")
        L0.cleared = [(cleared, 6)]

        def clear(pool):
            prelude.done(pool)
            prelude.bonus_done(pool)
            for buf in (L0.tv_bd[:], L0.b_bd[:], L0.v_bd[:], L0.gt[:], L0.s_bd[:], L0.s[0]):
                pool.memset(buf, 0.0).then_inc(cleared, 1)
        k.phases.append(Phase(pool=clear))
        core = rwkv_core(k, z0, L0, lambda eng: (prelude.done(eng), prelude.bonus_done(eng)), sem)
        k.phases.append(core)

        def load_late(act):
            core.done(act)
            act.dma_start(L0.g2[:], dram["in_g2"]).then_inc(L0.late, 16)
        k.phases.append(Phase(act=load_late))
        rout = rwkv_out(k, L0, core.done, prelude.bonus_done, sem)
        k.phases.append(rout)

        def load_swa(act):
            rout.done(act)
            act.dma_start(S.dist[:], dram["c_swa_dist"]).then_inc(S.loaded2, 16)
            act.dma_start(S.mask[:], dram["c_swa_mask"]).then_inc(S.loaded2, 16)
            act.dma_start(S.nsink[:], dram["in_sinks"]).then_inc(S.loaded2, 16)
        k.phases.append(Phase(act=load_swa))
        swa_done = swa(k, z0, S, rout.done, sem)
        g = Product(k, "hy_out", KD, KD, k.x_hi, k.x_lo)
        k.phases.append(post_norm(k, g, mix_m, "mix_post0", sem, lambda pe: (rout.done(pe), swa_done(pe))))
        free, wait_x = g.end(), updated()
        free = feed_forward(k, "up0", "down0", ffn, "ffn_pre0", "ffn_post0", sem, wait_x, free, "conv0")
        wait_x = updated()
        N.w1v = w1v
        k.phases.append(pre_norm(k, "mix_pre1", sem, wait_x, free))
        ffn0_end = free

        def load_k(act):
            act.wait_ge(k.mm, ffn0_end)
            act.dma_start(N.w1k[:], dram["in_w1k"]).then_inc(N.loaded_k, 16)
            act.dma_start(N.w2k[:].rearrange("p (f n) -> p f n", f=2), dram["in_w2k"]).then_inc(N.loaded_k, 16)
            act.dma_start(N.pos_k[:], dram["in_pos_k"]).then_inc(N.loaded_k, 16)
        k.phases.append(Phase(act=load_k))
        nsa_in = kept_product(k, "nsa_in", 21, z1, lambda t: k.v("scale1", t), sem)
        k.phases.append(nsa_in)
        nsa_done = nsa(k, z1, N, nsa_in.done, dram, sem, lambda eng: eng.wait_ge(k.mm, nsa_in.g.end()))
        g = Product(k, "nsa_out", KD, KD, k.x_hi, k.x_lo)
        k.phases.append(post_norm(k, g, mix_m, "mix_post1", sem, nsa_done))
        free, wait_x = g.end(), updated()
        free = feed_forward(k, "up1", "down1", ffn, "ffn_pre1", "ffn_post1", sem, wait_x, free, "conv1")
        wait_x = updated()
        free = feed_forward(k, "f1up", "f1down", ffn, "f1_pre", "f1_post", sem, wait_x, free)
        wait_x = updated()
        k.phases.append(pre_norm(k, "mix_pre2", sem, wait_x, free))
        B.loaded, B.loaded_rel = sem("lru_loaded"), sem("rel_loaded")
        ffn_end = free

        def load_lru(act):
            act.wait_ge(k.mm, ffn_end)
            act.dma_start(B.wx[:].rearrange("p (b n) -> p b n", b=16), dram["in_lru_x"]).then_inc(B.loaded, 16)
            act.dma_start(B.wa[:].rearrange("p (b n) -> p b n", b=16), dram["in_lru_a"]).then_inc(B.loaded, 16)
            act.dma_start(B.table[:], dram["in_rel"]).then_inc(B.loaded_rel, 16)
            act.dma_start(B.pick[:], dram["c_pick"]).then_inc(B.loaded_rel, 16)
            act.dma_start(B.rmask[:], dram["c_rmask"]).then_inc(B.loaded_rel, 16)
        k.phases.append(Phase(act=load_lru))
        rel = bias_vectors(k, B, dram, sem)
        k.phases.append(rel)
        xr = lru_input(k, "xr", B, sem)
        k.phases.append(xr)
        scan = lru_scan(k, B, lambda eng: (xr.done(eng), rel.written(eng)), sem)
        k.phases.append(scan)
        yr = lru_gate(k, "yr", B, scan.done, sem)
        k.phases.append(yr)
        done = yr.done
        for s in range(SLOTS_H):
            prev = done
            proj = kept_product(k, f"qkv{s}", 9, B.z, lambda t: k.v("scale2", t), sem)
            own_dve = proj.dve
            proj.dve = lambda dve, f=own_dve, prev=prev: (prev(dve), f(dve))
            k.phases.append(proj)
            done = dilated(k, B, s, proj.done, dram, rel.written, sem)
        at_done = done
        merged = blend(k, ("at", "g0", "rec", "g1"), ((B.at_hi, B.at_lo), (k.x_hi, k.x_lo), (B.rec_hi, B.rec_lo), (k.x_hi, k.x_lo)),
                       B, lambda eng: (at_done(eng), yr.done(eng)), sem)
        k.phases.append(merged)
        g = Product(k, "out2", KD, KD, B.m_hi, B.m_lo)
        k.phases.append(post_norm(k, g, ffn.m, "mix_post2", sem, merged.done))
        free, wait_x = g.end(), updated()
        free = feed_forward(k, "f2up", "f2down", ffn, "f2_pre", "f2_post", sem, wait_x, free)
        wait_x = updated()

        block = ctx.enter_context(nc.Block())

        @block.sync
        def _(sp):
            sp.dma_start(vec[:], dram["in_vec"]).then_inc(loaded, 16)
            sp.dma_start(k.x[:], dram["in_x"]).then_inc(loaded, 16)
            sp.dma_start(const[:], dram["in_const"]).then_inc(loaded, 16)
            for ph in k.phases:
                ph.sp(sp)
            sp.wait_ge(k.x_updated, KD * k.update_events)
            sp.dma_start(out, k.x[:]).then_inc(stored, 16)
            sp.wait_ge(stored, 16)

        @block.scalar
        def _(act):
            act.wait_ge(set_up, 4)
            act.sem_inc(k.mm, PAIRS)
            for u in range(PAIRS):
                k.hi(act, u)
            for ph in k.phases:
                ph.act(act)

        @block.gpsimd
        def _(pool):
            pool.sem_inc(k.lo_done, SLOTS)
            for ph in k.phases:
                ph.pool(pool)

        @block.tensor
        def _(pe):
            pe.wait_ge(set_up, 4)
            pe.wait_ge(loaded, 48)
            for ph in k.phases:
                ph.pe(pe)

        @block.vector
        def _(dve):
            dve.memset(k.ones[:], 1.0).then_inc(set_up, 1)
            dve.memset(k.eps[:], EPS).then_inc(set_up, 1)
            dve.memset(k.gn_eps[:], GN_EPS).then_inc(set_up, 1)
            dve.wait_ge(loaded, 48)
            dve.scalar_tensor_tensor(out=k.keep_scale[:], in0=k.v("mu", 0, 20), scalar=1.0, in1=k.v("scale0", 0, 20),
                                     op0=ALU.subtract, op1=ALU.mult).then_inc(set_up, 1)
            dve.tensor_scalar(k.v("one_k_a", 0, 4), k.v("k_a", 0, 4), -1.0, 1.0, ALU.mult, ALU.add).then_inc(set_up, 1)
            for n in ("f1_post", "f2_post"):
                dve.tensor_scalar(k.v(n, 0, KD), k.v(n, 0, KD), 0.5, None, ALU.mult).then_inc(set_up, 1)
            dve.wait_ge(set_up, 7)
            dve.sem_inc(k.bank_free, BANKS)
            for ph in k.phases:
                ph.dve(dve)


def kernel(**inputs):
    import concourse.bacc as _bacc
    from concourse.bass_utils import run_bass_kernel_spmd as _run

    a = {n: np.asarray(v) for n, v in inputs.items()}

    def tiles(w):
        K, N = w.shape
        kt, nt = K // P, N // P
        upt = 2 if kt > NBMAX else 1
        nb = kt // upt
        return np.ascontiguousarray(w.reshape(upt, nb, P, nt, P).transpose(3, 0, 2, 1, 4).reshape(nt * upt, P, nb * P))

    def interleave(u, v):
        K, N = u.shape
        return np.stack([u.reshape(K, N // P, P), v.reshape(K, N // P, P)], 2).reshape(K, 2 * N)

    def vcols(v):
        return v.reshape(-1, P).T

    w, vecs = {}, {}
    for l in range(2):
        up = a["ffn_w_up"][l]
        w[f"up{l}"] = tiles(interleave(up[:, :D_FF], up[:, D_FF:]))
        w[f"down{l}"] = tiles(a["ffn_w_down"][l])
        for n in ("mix_pre", "mix_post", "ffn_pre", "ffn_post"):
            vecs[f"{n}{l}"] = vcols(a[n + "_g"][l])
        for j in range(3):
            vecs[f"conv{l}_w{j}"] = vcols(a["ffn_conv_w"][l, j])
        vecs[f"conv{l}_b"] = vcols(a["ffn_conv_b"][l])
    for n in (1, 2):
        w[f"f{n}up"] = tiles(interleave(a[f"ffn{n}_w_gate_2"][0], a[f"ffn{n}_w_up_2"][0]))
        w[f"f{n}down"] = tiles(a[f"ffn{n}_w_down_2"][0])
        vecs[f"f{n}_pre"] = vcols(a[f"ffn{n}_norm_pre_2"][0])
        vecs[f"f{n}_post"] = vcols(a[f"ffn{n}_norm_post_2"][0])
    w2 = a["w_in_2"][0]
    A = 12 * P
    qkv = w2[:, :3 * A].reshape(D, 3, GROUPS, SLOTS_H, P)
    for s in range(SLOTS_H):
        w[f"qkv{s}"] = tiles(qkv[:, :, :, s].transpose(0, 2, 1, 3).reshape(D, 9 * P))
    for j, n in enumerate(("xr", "yr", "g0", "g1")):
        w[n] = tiles(w2[:, 3 * A + j * D:3 * A + (j + 1) * D])
    w["at"], w["rec"], w["out2"] = (tiles(a[n][0]) for n in ("w_attn_branch_2", "w_rec_branch_2", "w_out_2"))
    vecs["scale2"] = np.broadcast_to(np.array([-P ** -0.5, 1.0, 1.0] * 3, np.float32)[None], (P, 9))
    vecs["mix_pre2"], vecs["mix_post2"] = vcols(a["mix_norm_pre_2"][0]), vcols(a["mix_norm_post_2"][0])
    for j in range(LRU_TAPS):
        vecs[f"lconv_w{j}"] = vcols(a["conv_w_2"][0, j])
    vecs["lconv_b"] = vcols(a["conv_b_2"][0])
    vecs["b_x"], vecs["b_a"] = vcols(a["lru_b_x_2"][0].reshape(-1)), vcols(a["lru_b_a_2"][0].reshape(-1))
    vecs["a_param"] = vcols(a["lru_a_param_2"][0])
    hy = a["hy_w_in"][0]
    q = hy[:, :512].reshape(D, 2, 4, HD).transpose(0, 2, 1, 3).reshape(D, 512)
    w["hy_in"] = tiles(np.concatenate([q, hy[:, 512:]], 1))
    w["hy_out"] = tiles(a["hy_w_out"][0])
    vecs["mu"] = vcols(np.concatenate([np.zeros(6 * P, np.float32), a["rwkv_mu"][0]]))
    vecs["scale0"] = np.broadcast_to(np.array([HD ** -0.5] * 4 + [-1.0] * 16, np.float32)[None], (P, 20))
    for n in ("w0", "a0", "k_k", "k_a", "ln_g", "ln_b"):
        vecs[n] = vcols(a["rwkv_" + n][0])
    vecs["r_k"] = vcols(a["rwkv_r_k"][0].reshape(-1))
    vecs["one_k_a"] = np.zeros((P, 4), np.float32)
    ni = a["nsa_w_in"][0]
    q = ni[:, :D].reshape(D, 2, 2, 4, HD).transpose(0, 1, 3, 2, 4).reshape(D, D)
    w["nsa_in"] = tiles(np.concatenate([q, ni[:, D:], np.zeros((D, 21 * P - ni.shape[1]), np.float32)], 1))
    w["nsa_out"] = tiles(a["nsa_w_out"][0])
    vecs["scale1"] = np.broadcast_to(np.array([-HD ** -0.5] * 8 + [1.0] * 13, np.float32)[None], (P, 21))
    shared, own = shape_constants()

    def pack(d):
        c, at = {}, 0
        for n, v in d.items():
            c[n] = at
            at += v.shape[1]
        return c, np.ascontiguousarray(np.concatenate(list(d.values()), 1))

    cols, vec = pack(vecs)
    ccols, const = pack(shared)
    arrays = {"in_vec": vec, "in_const": const}
    arrays["in_x"] = np.ascontiguousarray(a["x"][0].T.reshape(KD, P, T).transpose(1, 0, 2))
    arrays["in_wa2"] = np.concatenate([a["rwkv_w2"][0], a["rwkv_a2"][0]], 0)
    arrays["in_g2"] = a["rwkv_g2"][0]
    arrays["in_sinks"] = np.ascontiguousarray(np.broadcast_to(a["swa_sinks"][0][None], (P, 8)))
    for n in "kv":
        w1 = a[f"nsa_cmp_w1_{n}"][0].transpose(1, 0, 2).reshape(HD, CL * 2 * P)
        arrays[f"in_w1{n}"] = np.concatenate([w1, w1], 0)
        arrays[f"in_w2{n}"] = np.ascontiguousarray(a[f"nsa_cmp_w2_{n}"][0].reshape(2, P, HD).transpose(1, 0, 2))
        pos = a[f"nsa_cmp_pos_{n}"][0].T
        arrays[f"in_pos_{n}"] = np.concatenate([pos, pos], 0)
    for n in "xa":
        arrays[f"in_lru_{n}"] = np.ascontiguousarray(
            a[f"lru_w_{n}_2"][0].reshape(4, 2, P, 2, P).transpose(2, 0, 1, 3, 4).reshape(P, 16, P))
    arrays["in_rel"] = a["rel_bias_table_2"]
    arrays |= {"c_" + n: v for n, v in own.items()} | {"w_" + n: v for n, v in w.items()}
    nc = _bacc.Bacc("TRN2", target_bir_lowering=False, num_devices=1)
    dram = {n: nc.dram_tensor(n, v.shape, F32, kind="ExternalInput").ap() for n, v in arrays.items()}
    dram["rv"] = nc.dram_tensor("rel_vectors", (12, T + P), F32, kind="Internal").ap()
    out = nc.dram_tensor("out_x", (P, KD, T), F32, kind="ExternalOutput").ap()
    build(nc, dram, cols, ccols, out)
    r = _run(nc, [arrays], core_ids=[0])
    return np.ascontiguousarray(r.results[0]["out_x"].transpose(1, 0, 2).reshape(D, T).T)[None]
```
